# Optimizing a Trainium2 kernel written in Bass

```python
import math
import jax, jax.numpy as jnp
from jax import lax
import numpy as np

D_MODEL = 1024
BATCH = 1
SEQ = 256
DEPTH = 2

MLA_HEADS = 8
MLA_NOPE = 64
MLA_ROPE = 32
MLA_V = 64
MLA_Q_RANK = 384
MLA_KV_RANK = 256
DIFF_HEADS = 4
DIFF_HD = 64
DIFF_VD = 2 * DIFF_HD
CONV_CH = 512
CONV_K = 31
D_FF = 2816
FFN_CONV_K = 3
ROPE_THETA = 10000.0
Q_BLOCK = 128
NORM_EPS = 1e-6
N_BRANCH = 3
N_MOD = 6

DIFF_Q_COLS = DIFF_HEADS * 2 * DIFF_HD
DIFF_V_COLS = DIFF_HEADS * DIFF_VD
CONV_COLS = 2 * CONV_CH
GATE_COLS = N_BRANCH * D_MODEL
IN_SIZES = (MLA_Q_RANK, MLA_KV_RANK, MLA_ROPE, DIFF_Q_COLS, DIFF_Q_COLS, DIFF_V_COLS, CONV_COLS, GATE_COLS)
IN_COLS = sum(IN_SIZES)

kernel_name = 'hybrid_mla_diffattn_conformer_convffn_adaln'

def rms_norm(x, g):
    xf = x.astype(jnp.float32)
    y = xf * lax.rsqrt(jnp.mean(xf * xf, axis=-1, keepdims=True) + NORM_EPS)
    return (y * g.astype(jnp.float32)).astype(x.dtype)

def layer_norm(x, g, b):
    xf = x.astype(jnp.float32)
    mu = jnp.mean(xf, axis=-1, keepdims=True)
    xc = xf - mu
    var = jnp.mean(xc * xc, axis=-1, keepdims=True)
    return (xc * lax.rsqrt(var + NORM_EPS) * g.astype(jnp.float32) + b.astype(jnp.float32)).astype(x.dtype)

def rope_tables(positions, dim):
    inv = 1.0 / (ROPE_THETA ** (jnp.arange(0, dim, 2, dtype=jnp.float32) / dim))
    ang = positions.astype(jnp.float32)[..., None] * inv
    return jnp.cos(ang), jnp.sin(ang)

def apply_rope(x, cos, sin):
    shape = (cos.shape[0],) + (1,) * (x.ndim - 3) + cos.shape[1:]
    cs = cos.reshape(shape)
    sn = sin.reshape(shape)
    xf = x.astype(jnp.float32)
    x1, x2 = jnp.split(xf, 2, axis=-1)
    return jnp.concatenate([x1 * cs - x2 * sn, x2 * cs + x1 * sn], axis=-1).astype(x.dtype)

def causal_dwconv(x, w, b):
    k = w.shape[0]
    y = lax.conv_general_dilated(x, w[:, None, :].astype(x.dtype), window_strides=(1,), padding=[(k - 1, 0)],
                                 dimension_numbers=('NWC', 'WIO', 'NWC'), feature_group_count=x.shape[-1])
    return y + b.astype(x.dtype)

def causal_block_attention(q, k, v, scale, combine):
    bsz, g, m, s, dk = q.shape
    nb = s // Q_BLOCK
    qb = q.reshape(bsz, g, m, nb, Q_BLOCK, dk).transpose(3, 0, 1, 2, 4, 5)
    kpos = jnp.arange(s)

    def body(args):
        qi, i = args
        sc = jnp.einsum('bgmtd,bgmsd->bgmts', qi, k).astype(jnp.float32) * scale
        qpos = i * Q_BLOCK + jnp.arange(Q_BLOCK)
        mask = kpos[None, :] <= qpos[:, None]
        sc = jnp.where(mask, sc, jnp.finfo(jnp.float32).min)
        p = jax.nn.softmax(sc, axis=-1)
        w = combine(p).astype(v.dtype)
        return jnp.einsum('bgts,bgsd->bgtd', w, v)

    out = lax.map(body, (qb, jnp.arange(nb)))
    return out.transpose(1, 2, 0, 3, 4).reshape(bsz, g, s, v.shape[-1])

def token_mixer(h, cos_r, sin_r, cos_d, sin_d, lambda_init, w_in, q_norm_g, w_uq, kv_norm_g, w_ukv, w_out_mla,
                diff_lambda, diff_subln_g, w_out_diff, conv_dw_w, conv_dw_b, conv_ln_g, conv_ln_b, w_out_conv, w_o):
    bsz, s, _ = h.shape
    proj = h @ w_in
    q_lat, kv_lat, k_rope, dq, dk, dv, conv_in, gate_in = jnp.split(
        proj, np.cumsum(IN_SIZES)[:-1].tolist(), axis=-1)

    q = rms_norm(q_lat, q_norm_g) @ w_uq
    q = q.reshape(bsz, s, MLA_HEADS, MLA_NOPE + MLA_ROPE).transpose(0, 2, 1, 3)
    q_nope, q_pe = q[..., :MLA_NOPE], q[..., MLA_NOPE:]
    q_pe = apply_rope(q_pe, cos_r, sin_r)
    kv = rms_norm(kv_lat, kv_norm_g) @ w_ukv
    kv = kv.reshape(bsz, s, MLA_HEADS, MLA_NOPE + MLA_V).transpose(0, 2, 1, 3)
    k_nope, v_a = kv[..., :MLA_NOPE], kv[..., MLA_NOPE:]
    k_pe = apply_rope(k_rope[:, None], cos_r, sin_r)
    qa = jnp.concatenate([q_nope, q_pe], axis=-1)[:, :, None]
    ka = jnp.concatenate([k_nope, jnp.broadcast_to(k_pe, (bsz, MLA_HEADS, s, MLA_ROPE))], axis=-1)[:, :, None]
    o_a = causal_block_attention(qa, ka, v_a, 1.0 / math.sqrt(MLA_NOPE + MLA_ROPE), lambda p: p[:, :, 0])
    y_a = o_a.transpose(0, 2, 1, 3).reshape(bsz, s, MLA_HEADS * MLA_V) @ w_out_mla

    qd = apply_rope(dq.reshape(bsz, s, DIFF_HEADS, 2, DIFF_HD).transpose(0, 2, 3, 1, 4), cos_d, sin_d)
    kd = apply_rope(dk.reshape(bsz, s, DIFF_HEADS, 2, DIFF_HD).transpose(0, 2, 3, 1, 4), cos_d, sin_d)
    vd = dv.reshape(bsz, s, DIFF_HEADS, DIFF_VD).transpose(0, 2, 1, 3)
    dl = diff_lambda.astype(jnp.float32)
    lam = jnp.exp(jnp.sum(dl[0] * dl[1])) - jnp.exp(jnp.sum(dl[2] * dl[3])) + lambda_init
    o_b = causal_block_attention(qd, kd, vd, 1.0 / math.sqrt(DIFF_HD),
                                 lambda p: p[:, :, 0] - lam * p[:, :, 1])
    o_b = rms_norm(o_b, diff_subln_g) * (1.0 - lambda_init)
    y_b = o_b.transpose(0, 2, 1, 3).reshape(bsz, s, DIFF_HEADS * DIFF_VD) @ w_out_diff

    a, g = jnp.split(conv_in, 2, axis=-1)
    u = a * jax.nn.sigmoid(g)
    u = causal_dwconv(u, conv_dw_w, conv_dw_b)
    u = jax.nn.silu(layer_norm(u, conv_ln_g, conv_ln_b))
    y_c = u @ w_out_conv

    gates = jax.nn.sigmoid(gate_in).reshape(bsz, s, N_BRANCH, D_MODEL)
    merged = gates[:, :, 0] * y_a + gates[:, :, 1] * y_b + gates[:, :, 2] * y_c
    return merged @ w_o

def conv_gated_mlp(h, w_up, ffn_conv_w, ffn_conv_b, w_down):
    u = causal_dwconv(h @ w_up, ffn_conv_w, ffn_conv_b)
    a, b = jnp.split(u, 2, axis=-1)
    return (jax.nn.silu(a) * b) @ w_down

def setup_inputs(seed: int = 0) -> dict:
    key = jax.random.key(seed)
    ks = jax.random.split(key, 32)
    f32 = jnp.float32
    L, D = DEPTH, D_MODEL

    def dense(k, shape, fan_in, gain=1.0):
        return jax.random.normal(k, shape, f32) * (gain * fan_in ** -0.5)

    def gain_vec(k, shape):
        return 1.0 + 0.05 * jax.random.normal(k, shape, f32)

    def bias(k, shape):
        return 0.01 * jax.random.normal(k, shape, f32)

    x = jax.random.normal(ks[0], (BATCH, SEQ, D), f32)
    c = jax.random.normal(ks[1], (BATCH, D), f32)
    positions = (jnp.arange(SEQ, dtype=jnp.int32)[None, :]
                 + jax.random.randint(ks[2], (BATCH, 1), 0, 1024, dtype=jnp.int32))
    return {
        'x': x,
        'c': c,
        'positions': positions,
        'ada_w': dense(ks[3], (L, D, N_MOD * D), D, 0.5),
        'ada_b': bias(ks[4], (L, N_MOD * D)),
        'norm1_g': gain_vec(ks[5], (L, D)),
        'w_in': dense(ks[6], (L, D, IN_COLS), D),
        'q_norm_g': gain_vec(ks[7], (L, MLA_Q_RANK)),
        'w_uq': dense(ks[8], (L, MLA_Q_RANK, MLA_HEADS * (MLA_NOPE + MLA_ROPE)), MLA_Q_RANK),
        'kv_norm_g': gain_vec(ks[9], (L, MLA_KV_RANK)),
        'w_ukv': dense(ks[10], (L, MLA_KV_RANK, MLA_HEADS * (MLA_NOPE + MLA_V)), MLA_KV_RANK),
        'w_out_mla': dense(ks[11], (L, MLA_HEADS * MLA_V, D), MLA_HEADS * MLA_V),
        'diff_lambda': 0.1 * jax.random.normal(ks[12], (L, 4, DIFF_HD), f32),
        'diff_subln_g': gain_vec(ks[13], (L, DIFF_VD)),
        'w_out_diff': dense(ks[14], (L, DIFF_HEADS * DIFF_VD, D), DIFF_HEADS * DIFF_VD),
        'conv_dw_w': dense(ks[15], (L, CONV_K, CONV_CH), CONV_K),
        'conv_dw_b': bias(ks[16], (L, CONV_CH)),
        'conv_ln_g': gain_vec(ks[17], (L, CONV_CH)),
        'conv_ln_b': bias(ks[18], (L, CONV_CH)),
        'w_out_conv': dense(ks[19], (L, CONV_CH, D), CONV_CH),
        'w_o': dense(ks[20], (L, D, D), D),
        'norm2_g': gain_vec(ks[21], (L, D)),
        'w_up': dense(ks[22], (L, D, 2 * D_FF), D),
        'ffn_conv_w': dense(ks[23], (L, FFN_CONV_K, 2 * D_FF), FFN_CONV_K),
        'ffn_conv_b': bias(ks[24], (L, 2 * D_FF)),
        'w_down': dense(ks[25], (L, D_FF, D), D_FF),
        'final_g': gain_vec(ks[26], (D,)),
    }

def reference(x, c, positions, ada_w, ada_b, norm1_g, w_in, q_norm_g, w_uq, kv_norm_g, w_ukv, w_out_mla,
              diff_lambda, diff_subln_g, w_out_diff, conv_dw_w, conv_dw_b, conv_ln_g, conv_ln_b, w_out_conv, w_o,
              norm2_g, w_up, ffn_conv_w, ffn_conv_b, w_down, final_g):
    cos_r, sin_r = rope_tables(positions, MLA_ROPE)
    cos_d, sin_d = rope_tables(positions, DIFF_HD)
    cos_r, sin_r, cos_d, sin_d = (t.astype(x.dtype) for t in (cos_r, sin_r, cos_d, sin_d))
    c_act = jax.nn.silu(c)
    for l in range(DEPTH):
        lambda_init = 0.8 - 0.6 * math.exp(-0.3 * l)
        mod = (c_act @ ada_w[l] + ada_b[l])[:, None, :]
        sh1, sc1, gt1, sh2, sc2, gt2 = jnp.split(mod, N_MOD, axis=-1)
        h = rms_norm(x, norm1_g[l]) * (1.0 + sc1) + sh1
        x = x + gt1 * token_mixer(h, cos_r, sin_r, cos_d, sin_d, lambda_init, w_in[l], q_norm_g[l], w_uq[l],
                                  kv_norm_g[l], w_ukv[l], w_out_mla[l], diff_lambda[l], diff_subln_g[l],
                                  w_out_diff[l], conv_dw_w[l], conv_dw_b[l], conv_ln_g[l], conv_ln_b[l],
                                  w_out_conv[l], w_o[l])
        h = rms_norm(x, norm2_g[l]) * (1.0 + sc2) + sh2
        x = x + gt2 * conv_gated_mlp(h, w_up[l], ffn_conv_w[l], ffn_conv_b[l], w_down[l])
    return rms_norm(x, final_g)


_drawn_inputs = setup_inputs


def setup_inputs(seed=0):
    import zlib

    import numpy as np

    out = dict(_drawn_inputs(seed))
    spreads = {}
    factors = {'ada_b': 3.662,
     'norm1_g': 3.902,
     'q_norm_g': 8.0,
     'kv_norm_g': 8.0,
     'diff_lambda': 6.994,
     'diff_subln_g': 6.115,
     'conv_dw_b': 8.0,
     'conv_ln_g': 6.705,
     'conv_ln_b': 8.0,
     'ffn_conv_b': 8.0}
    for name, (base, spread) in spreads.items():
        noise = np.random.default_rng([zlib.crc32(name.encode()), seed]).standard_normal(out[name].shape)
        drawn = base * np.exp(spread * noise) if base else spread * noise
        out[name] = __import__('jax').numpy.asarray(drawn.astype(out[name].dtype))
    for name, factor in factors.items():
        out[name] = (out[name] * factor).astype(out[name].dtype)
    return out
```

```python
import math
from contextlib import ExitStack

import concourse.bass as bass
import numpy as np
from concourse import mybir

F32 = mybir.dt.float32
F32R = mybir.dt.float32r
BF16 = mybir.dt.bfloat16
I32 = mybir.dt.int32
ALU = mybir.AluOpType
ACT = mybir.ActivationFunctionType
AX = mybir.AxisListType

P = 128
LAYERS, D, T = 2, 1024, 256
DT = D // P
HEADS_M, NOPE, ROPE, QR, KVR = 8, 64, 32, 384, 256
QT, KVT = QR // P, KVR // P
HEADS_D, HD = 4, 64
CONV_CH, TAPS = 512, 31
CT = CONV_CH // P
FF, FTAPS = 2816, 3
FT = FF // P
EPS = 1e-6
SCALE_M = 1.0 / math.sqrt(NOPE + ROPE)
SCALE_D = 1.0 / math.sqrt(HD)
MASKED = -1e30

COL_K_ROPE = QR + KVR
COL_DQ = COL_K_ROPE + ROPE
COL_DK = COL_DQ + 2 * HEADS_D * HD
COL_DV = COL_DK + 2 * HEADS_D * HD
COL_CONV_A = COL_DV + 2 * HEADS_D * HD
COL_CONV_G = COL_CONV_A + CONV_CH
COL_GATE = COL_CONV_G + CONV_CH

LAT = 0
DIFF = LAT + 3
MLA = DIFF + 5 * 2
OUTS = MLA + 5 * 4
WO = OUTS + 6
UP = WO + 4
DOWN = UP + 2 * FF // 256
CHUNKS = DOWN + FT // 2
RAW = 4
SHARE = 3
SLOT = 2048
UP_LOOPS = 4
assert CHUNKS % RAW == 0 and LAYERS == 2

PB_DIFF, PB_MLA, PB_OUTS, PB_WO, PB_UP = 4, 12, 32, 44, 48
PB_USES = PB_UP + 22

TR_USES = ["Rq0", "Rkr", "Rk0", "TD0", "Rq1", "TD1", "Rk1", "TD2", "TD3", "RM0", "TM0A", "TM0B", "RM1",
           "TM1A", "TM1B", "RM2", "TM2A", "TM2B", "RM3", "TM3A", "TM3B"]
OB_USES = ["V0", "PD0", "V1", "PD1", "VM0", "PD2", "PD3", "VM1", "PM0A", "PM0B", "VM2", "PM1A", "PM1B",
           "VM3", "PM2A", "PM2B", "PM3A", "PM3B"]
ST_USES = ["N1", "LAT", "SUB0", "SUB1", "LNS", "LNQ", "N2"]
SC_USES = ["D0", "D1", "D2", "D3", "M0", "M1", "M2", "M3"]

ROPED = ["Rq0", "Rk0", "Rq1", "Rk1", "RM0", "RM1", "RM2", "RM3"]

SCORES_AT = {6: "D0", 8: "D1", 11: "D2", 13: "D3", 16: "M0", 21: "M1", 26: "M2", 31: "M3"}
TRANSPOSE_AT = {8: "TD0", 10: "TD1", 13: "TD2", 15: "TD3", 18: "TM0A", 19: "TM0B", 23: "TM1A", 24: "TM1B",
                28: "TM2A", 29: "TM2B", 33: "TM3A", 34: "TM3B"}
VALUES_AT = {9: "PD0", 11: "PD1", 14: "PD2", 16: "PD3", 19: "PM0A", 20: "PM0B", 24: "PM1A", 25: "PM1B",
             29: "PM2A", 30: "PM2B", 34: "PM3A", 35: "PM3B"}
ROTATE_AT = {4: ["Rq0", "Rkr"], 5: ["Rk0"], 9: ["Rq1"], 10: ["Rk1"], 15: ["RM0"], 20: ["RM1"], 25: ["RM2"],
             30: ["RM3"]}
STATS_AT = {3: "LAT", 17: "SUB0", 19: "SUB1", 24: "LNS", 26: "LNQ"}
TAPS_AT = {8: (0, 1, 7), 9: (0, 7, 13), 10: (0, 13, 19), 11: (0, 19, 25), 12: (0, 25, 31),
           13: (1, 1, 4), 14: (1, 4, 7), 15: (1, 7, 11), 16: (1, 11, 15), 17: (1, 15, 20), 20: (1, 20, 24),
           21: (1, 24, 28), 22: (1, 28, 31)}

ADA_PART = 4
ADA_PARTS = [2, 3, 4, 5, 0, 1]
ADA_STEPS = [1, 4, 7, 10, 14, 17, 20, 23, 27, 30, 33, 36] + [None] * 4 + [60, 62, 64, 66, 68, 70, 72, 74]
ADA_LOADS = [min(n + (1 if n < UP else 2), CHUNKS - 1) if n else None for n in ADA_STEPS]
ADA_LOOP, ADA_NEXT = 12, 16
ADA_REDUCE_AT = {12: 0, 25: 1, 38: 2, UP + 4 * UP_LOOPS: 3, 67: 4, 75: 5}
ADA_CHUNKS = len(ADA_STEPS)
ADA_FIRST = 2 * ADA_PART
assert UP_LOOPS == ADA_PART and UP + 4 * UP_LOOPS == 59

V_N1, V_N2, V_ADAB, V_QG, V_KVG, V_CB, V_LNG, V_LNB, V_SUB, V_FB = 0, 8, 16, 64, 67, 69, 73, 77, 81, 82
ROWS_A = V_FB + 2 * FT
V_CW = ROWS_A
ROWS_B = TAPS * CT
V_FW = V_CW + ROWS_B
V_LAM = V_FW + FTAPS * 2 * FT
NV = V_LAM + 2
C_ID, C_RD, C_RM, C_INV, C_LAM = 0, 128, 256, 352, 354
C_MASK = C_LAM + 2 * LAYERS
NC_CONST = C_MASK + 384

TWO_PI_1, TWO_PI_2 = 6.28125, 0.0019350051879882812
TWO_PI_3 = 2 * math.pi - TWO_PI_1 - TWO_PI_2
ROUND = 1.5 * 2.0**23


def constants():
    c = np.zeros((P, NC_CONST), np.float32)
    c[:, C_ID:C_ID + P] = np.eye(P)
    for base in (0, HD):
        for i in range(HD // 2):
            c[base + i + HD // 2, C_RD + base + i] = -1.0
            c[base + i, C_RD + base + i + HD // 2] = 1.0
    for i in range(ROPE // 2):
        c[NOPE + i + ROPE // 2, C_RM + NOPE + i] = -1.0
        c[NOPE + i, C_RM + NOPE + i + ROPE // 2] = 1.0
    later = np.triu(np.full((P, P), MASKED, np.float32), 1)
    c[:, C_MASK:C_MASK + P] = later
    c[:, C_MASK + 2 * P:C_MASK + 3 * P] = later
    inv = lambda dim: 1.0 / (np.float32(10000.0) ** (np.arange(0, dim, 2, dtype=np.float32) / np.float32(dim)))
    c[:, C_INV] = np.tile(inv(HD), 4)
    c[NOPE:NOPE + ROPE, C_INV + 1] = np.tile(inv(ROPE), 2)
    for l in range(LAYERS):
        init = 0.8 - 0.6 * math.exp(-0.3 * l)
        c[:, C_LAM + 2 * l] = init
        c[:, C_LAM + 2 * l + 1] = 1.0 - init
    return c


V_LINKS, V_LINKS_UP = 133, 6
FREE = 1
VEC_LOADS = LAYERS * 13


def chunk_size(n):
    if n == LAT + 2:
        return DT * (P + ROPE)
    if MLA <= n < OUTS and (n - MLA) % 5 == 0:
        return QT * 192
    if MLA <= n < OUTS and (n - MLA) % 5 == 1:
        return KVT * 256
    return SLOT


def gate_of(n):
    p, r = divmod(n - MLA, 5)
    return 3 * p + r - 2 if MLA <= n < OUTS and r >= 2 else None


def last_use(n):
    if n < MLA:
        if n < DIFF:
            return "pb", n + 1 + (n == LAT + 2)
        i, what = divmod(n - DIFF, 5)
        if what == 2:
            return "ob", OB_USES.index(f"V{i}") + 1
        return "pb", PB_DIFF + 4 * i + (what if what < 2 else what - 1) + 1
    if n < OUTS:
        p, what = divmod(n - MLA, 5)
        return ("ob", OB_USES.index(f"VM{p}") + 1) if what == 1 else ("pb", PB_MLA + 5 * p + what + 1)
    if n < WO:
        return "pb", PB_OUTS + 2 * (n - OUTS) + 2
    return "pb", PB_WO + n - WO + 1


class Chain:

    def __init__(self, eng, sem):
        self.eng, self.sem, self.n, self.base = eng, sem, 0, 0

    def link(self, ins):
        ins.then_inc(self.sem, 1)
        self.n += 1
        self.eng.wait_ge(self.sem, self.base + self.n)


def trunk_kernel(nc, x, c, positions, ada_w, ada_b, norm1_g, w_in, q_norm_g, w_uq, kv_norm_g, w_ukv, w_out_mla,
                 diff_lambda, diff_subln_g, w_out_diff, conv_dw_w, conv_dw_b, conv_ln_g, conv_ln_b, w_out_conv,
                 w_o, norm2_g, w_up, ffn_conv_w, ffn_conv_b, w_down, final_g, consts, out):
    stack = ExitStack()
    with stack:
        def sb(name, shape, dt=F32, where=stack):
            return where.enter_context(nc.sbuf_tensor(name, shape, dt))

        def bank(name):
            return stack.enter_context(nc.psum_tensor(name, [P, 512], F32))

        def sem(name):
            return stack.enter_context(nc.semaphore(name))

        xT = sb("xT", [P, DT, T])
        xn = sb("xn", [P, DT, T])
        buf = sb("buf", [P, DT, T])
        hH = sb("hH", [P, DT, T], F32R)
        hL = sb("hL", [P, DT, T], F32R)
        loaded = ExitStack()
        raw = [sb(f"raw{i}", [P, SLOT], F32, loaded) for i in range(RAW)]
        loaded.close()
        wL = [sb(f"wL{i}", [P, SLOT], F32R) for i in range(RAW)]
        wH = [sb(f"wH{i}", [P, SLOT], F32R) for i in range(RAW)]
        ada = sb("ada", [P, 2, 1024])
        acc = sb("acc", [P, 1024])
        cst = sb("cst", [P, C_MASK])
        maskb = sb("maskb", [P, 384], BF16)
        identb = sb("identb", [P, P], BF16)
        ones = sb("ones", [P, P])
        eps = sb("eps", [P, 1])
        vec_all = sb("vec_all", [P, LAYERS, NV])
        vec = sb("vec", [P, NV])
        fin_g = sb("fin_g", [P, DT])
        c_act = sb("c_act", [P, 3, DT])
        mod = sb("mod", [P, 6 * DT])
        gs = sb("gs", [P, 2, DT])
        lamb = sb("lamb", [P, 2, LAYERS])
        sub_g = sb("sub_g", [P, 1])
        lam_now = sb("lam_now", [P, 1])
        half_b = sb("half_b", [P, CT])
        cos = sb("cos", [P, 2, T])
        sin = sb("sin", [P, 2, T])
        rdev = sb("rdev", [P, 512])
        ident = cst[:, C_ID:C_ID + P]

        first = ExitStack()
        rows = sb("rows", [P, 9, P], F32, first)
        lam_in = sb("lam_in", [P, LAYERS, 4, HD], F32, first)
        lam_p = sb("lam_p", [P, LAYERS, 2, HD], F32, first)
        lam_s = sb("lam_s", [P, LAYERS, 2], F32, first)
        mask = sb("mask", [P, 384], F32, first)
        ang = sb("ang", [P, 2, T], F32, first)
        turns = sb("turns", [P, 2, T], F32, first)
        pos_i = turns[:, 1, :].bitcast(I32)
        ada_pre = sb("ada_pre", [P, ADA_FIRST, 2, 1024], F32, first)
        first.close()

        mix = ExitStack()
        G = sb("G", [P, 24, T], F32, mix)
        latq = sb("latq", [P, QT + KVT, T], F32, mix)
        latH = sb("latH", [P, QT + KVT, T], F32R, mix)
        latL = sb("latL", [P, QT + KVT, T], F32R, mix)
        qraw = sb("qraw", [P, 2, T], F32, mix)
        rot_s = sb("rot_s", [P, 2, T], F32, mix)
        qD = sb("qD", [P, 2, T], F32, mix)
        kM = sb("kM", [P, 2, T], F32, mix)
        vM = [sb(f"vM{i}", [P, 2, P], F32, mix) for i in range(2)]
        W = sb("W", [P, 2, 384], F32, mix)
        PT = sb("PT", [P, 384], F32, mix)
        nmax = sb("nmax", [P, 4], F32, mix)
        nb = sb("nb", [P, 4], F32, mix)
        esum = sb("esum", [P, 4], F32, mix)
        rsum = sb("rsum", [P, 4], F32, mix)
        oBH = sb("oBH", [P, HEADS_D, T], F32R, mix)
        oBL = sb("oBL", [P, HEADS_D, T], F32R, mix)
        oAH = sb("oAH", [P, HEADS_M // 2, T], F32R, mix)
        oAL = sb("oAL", [P, HEADS_M // 2, T], F32R, mix)
        uH = sb("uH", [P, CT, T], F32R, mix)
        uL = sb("uL", [P, CT, T], F32R, mix)
        mix.close()
        lat = buf[:, 0:QT + KVT, :]
        cv = buf[:, 0:CT, :]
        oB = buf[:, CT:CT + HEADS_D, :]
        ln_th = buf[:, CT:2 * CT, :]
        oBq = latq[:, 0:HEADS_D, :]
        flat_xn = xn[:, :, :].rearrange("p k t -> p (k t)")
        vD = [flat_xn[:, i * 512:(i + 1) * 512].rearrange("p (k t) -> p k t", k=2) for i in range(2)]
        E = flat_xn[:, 1024:1024 + 768].rearrange("p (m s) -> p m s", m=2)
        late = G[:, 12:24, :].rearrange("p k t -> p (k t)")
        kraw = late[:, 0:512].rearrange("p (k t) -> p k t", k=2)
        kD = late[:, 512:1024].rearrange("p (k t) -> p k t", k=2)
        cth = late[:, 1024:1536].rearrange("p (k t) -> p k t", k=2)
        krope = late[:, 1536:1536 + T]
        up_pad = late[:, 1792:1792 + CT * (TAPS - 1 + T)].rearrange("p (k t) -> p k t", k=CT)
        qM = qD
        mlp = ExitStack()
        gH = sb("gH", [P, FT, T], F32R, mlp)
        gL = sb("gL", [P, FT, T], F32R, mlp)
        ca = sb("ca", [P, 2, T], F32, mlp)
        cb = sb("cb", [P, 2, T], F32, mlp)
        th = sb("th", [P, 2, T], F32, mlp)
        gy = sb("gy", [P, 2, T], F32, mlp)
        mlp.close()

        PB = [bank("PB0"), bank("PB1")]
        SC = [bank("SC0"), bank("SC1")]
        TR = bank("TR")
        OB = bank("OB")
        ST = bank("ST")
        MI = bank("MI")
        DN = [SC[0], SC[1], TR, OB]
        OUT = [PB, SC]

        s_cst, s_x, s_pos, s_lam, s_vec = sem("cst_in"), sem("x_in"), sem("pos_in"), sem("lam_in_s"), sem("vec_in")
        raw_in = [sem(f"raw_in{i}") for i in range(RAW)]
        w_hi = sem("w_hi")
        w_lo = [sem(f"w_lo{i}") for i in range(RAW)]
        w_lo_pool = [sem(f"w_lo_pool{i}") for i in range(RAW)]
        pb_full, pb_read = sem("pb_full"), [sem("pb_read0"), sem("pb_read1")]
        tr_full, tr_read = sem("tr_full"), sem("tr_read")
        ob_full, ob_read = sem("ob_full"), sem("ob_read")
        st_full, st_read = sem("st_full"), sem("st_read")
        mi_full, mi_read = sem("mi_full"), sem("mi_read")
        sc_full, e_ready = sem("sc_full"), sem("e_ready")
        ada_in, ada_used, ada_half = sem("ada_in"), sem("ada_used"), sem("ada_half")
        ada_pre_in = [sem(f"ada_pre_in{i}") for i in range(ADA_FIRST)]
        acc_clear, v_link = sem("acc_clear"), sem("v_link")
        s_const, s_xtr, s_xt, s_vtr, s_vt = sem("const_made"), sem("x_turned"), sem("xT_made"), sem("vec_turned"), sem("vecs_made")
        s_cth, s_ang, s_table, s_lame, s_lamx = sem("c_tanh"), sem("angles"), sem("tables"), sem("lam_sums"), sem("lam_exp")
        x_ready, sq_ready, xn_ready, h_hi, h_lo = sem("x_ready"), sem("sq_ready"), sem("xn_ready"), sem("h_hi"), sem("h_lo")
        lat_y, lat_hi, lat_lo = sem("lat_y"), sem("lat_hi"), sem("lat_lo")
        roped, nb_ready, w_ready = sem("roped"), sem("nb_ready"), sem("w_ready")
        o_hi, sub_y, sub_hi, sub_lo = sem("o_hi"), sem("sub_y"), sem("sub_hi"), sem("sub_lo")
        conv_done, cen_ready, cen_sq, ln_y, ln_t, ln_u, ln_hi, ln_lo = (
            sem(n) for n in ("conv_done", "centred", "centred_sq", "ln_y", "ln_t", "ln_u", "ln_hi", "ln_lo"))
        m_ready, m_hi, m_lo = sem("merged"), sem("merged_hi"), sem("merged_lo")
        tap_ready, th_ready, gy_ready, g_hi, g_lo = (
            sem(n) for n in ("up_tap", "up_tanh", "up_gated", "gated_hi", "gated_lo"))
        down_used, fin_y, out_turned, s_out = (sem(n) for n in ("down_used", "fin_y", "out_turned", "out_done"))
        down_done, s_silu, s_cvec = sem("down_done"), sem("silu_c"), sem("c_in")
        out_ready = [sem("out_ready0"), sem("out_ready1")]

        def vector_share(n):
            return chunk_size(n) * SHARE // 8

        block = stack.enter_context(nc.Block())

        @block.sync
        def _(sp):
            sp.sem_inc(down_used, RAW)
            for s in (*pb_read, ob_read, tr_read, st_read, e_ready, gy_ready):
                sp.sem_inc(s, FREE)
            in_v = w_in.rearrange("l (k p) c -> l p k c", p=P)
            uq_v = w_uq.rearrange("l (k p) c -> l p k c", p=P)
            ukv_v = w_ukv.rearrange("l (k p) c -> l p k c", p=P)
            outs_v = [w.rearrange("l (k p) c -> l p k c", p=P) for w in (w_out_conv, w_out_diff, w_out_mla)]
            wo_v = w_o.rearrange("l (k p) c -> l p k c", p=P)
            up_v = w_up.rearrange("l (k p) c -> l p k c", p=P)
            down_v = w_down.rearrange("l (k p) c -> l p k c", p=P)
            ada_v = ada_w.rearrange("l (k p) c -> p (l k) c", p=P)

            def load(l, n, r=0):
                s = n % RAW
                if n < RAW:
                    sp.wait_ge(down_used, RAW + l * (FT // 2) + n - RAW + 1)
                elif n - RAW >= DOWN:
                    sp.wait_ge(down_used, RAW + l * (FT // 2) + n - RAW - DOWN + 1)
                else:
                    where, count = last_use(n - RAW)
                    if where == "pb":
                        sp.wait_ge(pb_full, l * PB_USES + count + 4 * r)
                    else:
                        sp.wait_ge(ob_full, l * len(OB_USES) + count)
                if n < LAT + 2:
                    src = in_v[l, :, :, n * 256:(n + 1) * 256]
                elif n == LAT + 2:
                    src = in_v[l, :, :, 512:512 + P + ROPE]
                elif n < MLA:
                    i, what = divmod(n - DIFF, 5)
                    col = (COL_DQ, COL_DK, COL_DV, COL_CONV_G, COL_CONV_A)[what] + 256 * i
                    src = in_v[l, :, :, col:col + 256]
                elif n < OUTS:
                    p, what = divmod(n - MLA, 5)
                    g = gate_of(n)
                    if what == 0:
                        src = uq_v[l, :, :, 192 * p:192 * (p + 1)]
                    elif what == 1:
                        src = ukv_v[l, :, :, 256 * p:256 * (p + 1)]
                    else:
                        src = in_v[l, :, :, COL_GATE + 256 * g:COL_GATE + 256 * (g + 1)]
                elif n < WO:
                    b, half = divmod(n - OUTS, 2)
                    src = outs_v[b][l, :, :, 512 * half:512 * (half + 1)]
                elif n < UP:
                    src = wo_v[l, :, :, 256 * (n - WO):256 * (n - WO + 1)]
                elif n < DOWN:
                    i, b = divmod(n - UP, 2)
                    src = up_v[l, :, :, bass.ds(r * 512 + (i * 256 + b * FF), 256)]
                else:
                    src = down_v[l, :, 2 * (n - DOWN):2 * (n - DOWN) + 2, :]
                k, w = src.shape[-2], src.shape[-1]
                sp.dma_start(raw[s][:, 0:k * w].rearrange("p (k c) -> p k c", k=k), src).then_inc(raw_in[s], 16)

            def load_ada(l, a, r=0):
                part, i = ADA_PARTS[a // ADA_PART], a % ADA_PART
                sp.wait_ge(ada_used, ADA_FIRST + l * ADA_CHUNKS + a + r)
                if a < ADA_NEXT:
                    src = ada_v[:, bass.ds(l * DT + 2 * r + 2 * i, 2), 1024 * part:1024 * (part + 1)]
                else:
                    src = ada_v[:, (LAYERS - 1) * DT + 2 * i:(LAYERS - 1) * DT + 2 * i + 2,
                                1024 * part:1024 * (part + 1)]
                sp.dma_start(ada[:, :, :], src).then_inc(ada_in, 16)

            sp.dma_start(xn[:, :, :].rearrange("p (a k) t -> p a (k t)", a=2),
                         x[0, :, :].rearrange("(a p) d -> p a d", p=P)).then_inc(s_x, 16)
            for a in range(ADA_FIRST):
                part, i = divmod(a, ADA_PART)
                sp.dma_start(ada_pre[:, a, :, :],
                             ada_v[:, 2 * i:2 * i + 2, 1024 * part:1024 * (part + 1)]).then_inc(ada_pre_in[a], 16)

            def ada_behind(l, n):
                if n not in ADA_LOADS:
                    return
                a = ADA_LOADS.index(n)
                if a < ADA_NEXT:
                    load_ada(l, a)
                else:
                    with sp.If(l < LAYERS - 1):
                        load_ada(l, a)

            with sp.Fori(0, LAYERS) as l:
                for n in range(UP):
                    load(l, n)
                    ada_behind(l, n)
                with sp.Fori(0, UP_LOOPS) as r:
                    for j in range(4):
                        load(l, UP + j, r)
                    load_ada(l, ADA_LOOP, r)
                for n in range(UP + 4 * UP_LOOPS, CHUNKS):
                    load(l, n)
                    ada_behind(l, n)

            for a in range(2):
                sp.wait_ge(out_ready[a], 2)
                sp.dma_start(out[0, a * P:(a + 1) * P, :],
                             xn[:, 4 * a:4 * a + 4, :].rearrange("p k t -> p (k t)")).then_inc(s_out, 16)
            sp.wait_ge(s_out, 32)

        def factors(i):
            return c_act[:, 2, 2 * i:2 * i + 2]

        @block.gpsimd
        def _(pool):
            def low(l, n, r=0):
                s, cut, size = n % RAW, vector_share(n), chunk_size(n)
                pool.wait_ge(w_hi, l * CHUNKS + n + 1 + 4 * r)
                pool.tensor_tensor(wL[s][:, cut:size], raw[s][:, cut:size], wH[s][:, cut:size].bitcast(F32),
                                   ALU.subtract).then_inc(w_lo_pool[s], 1)

            with pool.Fori(0, LAYERS) as l:
                for n in range(UP + 2):
                    low(l, n)
                with pool.Fori(0, UP_LOOPS) as r:
                    for j in range(4):
                        low(l, UP + 2 + j, r)
                for n in range(UP + 4 * UP_LOOPS + 2, CHUNKS):
                    low(l, n)

        @block.scalar
        def _(act):
            act.dma_start(cst[:, :], consts[:, 0:C_MASK]).then_inc(s_cst, 16)
            act.dma_start(mask[:, :], consts[:, C_MASK:NC_CONST]).then_inc(s_cst, 16)
            act.dma_start(rows[0:DT, 8, :], c[0, :].rearrange("(k p) -> k p", p=P)).then_inc(s_cvec, 16)
            act.dma_start(rows[DT:2 * DT, 8, :], final_g.rearrange("(k p) -> k p", p=P)).then_inc(s_cvec, 16)
            act.dma_start(pos_i[:, :], positions.broadcast_to([P, T])).then_inc(s_pos, 16)
            act.dma_start(lam_in[:, :, :, :].rearrange("p l a b -> p (l a b)"),
                          diff_lambda.rearrange("(o l) a b -> o (l a b)", o=1).broadcast_to([P, LAYERS * 4 * HD])).then_inc(s_lam, 16)
            vec_rows = ((V_N1, norm1_g), (V_N2, norm2_g), (V_ADAB, ada_b), (V_QG, q_norm_g), (V_KVG, kv_norm_g),
                        (V_CB, conv_dw_b), (V_LNG, conv_ln_g), (V_LNB, conv_ln_b), (V_SUB, diff_subln_g),
                        (V_FB, ffn_conv_b))
            loads = 0
            for l in range(LAYERS):
                for at, v in vec_rows:
                    act.dma_start(rows[at:at + v.shape[1] // P, 4 * l, :],
                                  v[l, :].rearrange("(k p) -> k p", p=P)).then_inc(s_vec, 16)
                act.dma_start(rows[0:ROWS_B, 4 * l + 1, :], conv_dw_w[l].rearrange("k (c p) -> (k c) p", p=P)).then_inc(s_vec, 16)
                act.dma_start(rows[0:4 * FT, 4 * l + 2, :],
                              ffn_conv_w[l, 0:2, :].rearrange("k (c p) -> (k c) p", p=P)).then_inc(s_vec, 16)
                act.dma_start(rows[0:2 * FT, 4 * l + 3, :],
                              ffn_conv_w[l, 2, :].rearrange("(c p) -> c p", p=P)).then_inc(s_vec, 16)
                loads += len(vec_rows) + 3
            assert loads == VEC_LOADS

            act.wait_ge(s_vt, 1)
            act.activation(c_act[:, 1, :], c_act[:, 0, :], ACT.Tanh, scale=0.5).then_inc(s_cth, 1)
            act.wait_ge(s_lame, 1)
            act.activation(lam_s[:, :, :], lam_s[:, :, :], ACT.Exp).then_inc(s_lamx, 1)
            act.wait_ge(s_ang, 1)
            act.activation(sin[:, :, :], ang[:, :, :], ACT.Sin)
            act.activation(cos[:, :, :], turns[:, :, :], ACT.Sin).then_inc(s_table, 1)

            def high(l, n, r=0):
                s, size = n % RAW, chunk_size(n)
                act.wait_ge(raw_in[s], (l * (CHUNKS // RAW) + n // RAW + 1 + r) * 16)
                act.activation(wH[s][:, 0:size], raw[s][:, 0:size], ACT.Copy).then_inc(w_hi, 1)

            def full(l, u, r=0):
                act.wait_ge(pb_full, l * PB_USES + u + 1 + 4 * r)
                return PB[u % 2]

            def st_done(l, use):
                act.wait_ge(st_full, l * len(ST_USES) + ST_USES.index(use) + 1)

            def norm(l, which):
                for k in range(DT):
                    if which == 0:
                        act.wait_ge(x_ready, l * DT + k + 1)
                    elif k % 2 == 0:
                        u = PB_WO + k // 2
                        act.wait_ge(pb_read[u % 2], FREE + l * (PB_USES // 2) + u // 2 + 1)
                    act.activation(buf[:, k, :], xT[:, k, :], ACT.Square).then_inc(sq_ready, 1)
                st_done(l, ("N1", "N2")[which])
                act.activation(rdev[:, 0:T], ST[:, 0:T], ACT.Sqrt, bias=eps[:, :], scale=1.0 / D).then_inc(st_read, 1)
                for k in range(DT):
                    act.wait_ge(xn_ready, l * 2 * DT + which * DT + k + 1)
                    shift = mod[:, 3 * which * DT + k:3 * which * DT + k + 1]
                    act.activation(hH[:, k, :], xn[:, k, :], ACT.Identity, bias=shift).then_inc(h_hi, 1)

            def exps(l, use):
                act.wait_ge(nb_ready, l * len(SC_USES) + SC_USES.index(use) + 1)
                scale = SCALE_D if use[0] == "D" else SCALE_M
                for m in range(2):
                    for b, (lo, hi) in enumerate(((0, 128), (128, 384))):
                        i = 2 * m + b
                        ins = act.activation(E[:, m, lo:hi], SC[m][:, lo:hi], ACT.Exp, bias=nb[:, i:i + 1], scale=scale,
                                             accum_out=esum[:, i:i + 1])
                ins.then_inc(e_ready, 1)

            def mixer_step(l, n):
                high(l, n + 2)
                if n < LAT + 3:
                    m = 1 if n == 2 else 2
                    b = full(l, n)
                    src = b[:, 0:m * T].rearrange("p (k t) -> p k t", k=m)
                    act.activation(lat[:, 2 * n:2 * n + m, :], src, ACT.Copy)
                    act.activation(latq[:, 2 * n:2 * n + m, :], src, ACT.Square).then_inc(pb_read[n % 2], 1)
                    if n == 2:
                        b = full(l, 3)
                        act.activation(krope[0:96, :], b[0:96, 0:T], ACT.Copy).then_inc(pb_read[1], 1)
                elif n < MLA:
                    i, what = divmod(n - DIFF, 5)
                    if what in (0, 1):
                        b = full(l, PB_DIFF + 4 * i + what)
                        act.activation((qraw, kraw)[what][:, :, :].rearrange("p k t -> p (k t)"), b[:, :],
                                       ACT.Copy).then_inc(pb_read[what], 1)
                    elif what == 2:
                        act.wait_ge(ob_full, l * len(OB_USES) + OB_USES.index(f"V{i}") + 1)
                        act.activation(vD[i][:, :, :].rearrange("p k t -> p (k t)"), OB[:, :], ACT.Copy).then_inc(ob_read, 1)
                    elif what == 3:
                        b = full(l, PB_DIFF + 4 * i + 2)
                        act.activation(cth[:, :, :].rearrange("p k t -> p (k t)"), b[:, :], ACT.Tanh,
                                       scale=0.5).then_inc(pb_read[0], 1)
                elif n < OUTS:
                    p, what = divmod(n - MLA, 5)
                    u = PB_MLA + 5 * p + what
                    if what == 0:
                        b = full(l, u)
                        act.activation(qraw[0:96, :, :].rearrange("p k t -> p (k t)"), b[0:96, :],
                                       ACT.Copy).then_inc(pb_read[u % 2], 1)
                    elif what == 1:
                        b = full(l, u)
                        act.activation(kM[0:NOPE, :, :].rearrange("p k t -> p (k t)"), b[0:NOPE, :],
                                       ACT.Copy).then_inc(pb_read[u % 2], 1)
                        act.wait_ge(ob_full, l * len(OB_USES) + OB_USES.index(f"VM{p}") + 1)
                        act.activation(vM[p % 2][:, :, :].rearrange("p k t -> p (k t)"), OB[:, 0:256],
                                       ACT.Copy).then_inc(ob_read, 1)
                    else:
                        b, g = full(l, u), gate_of(n)
                        act.activation(G[:, 2 * g:2 * g + 2, :].rearrange("p k t -> p (k t)"), b[:, :], ACT.Tanh,
                                       scale=0.5).then_inc(pb_read[u % 2], 1)
                if n in VALUES_AT:
                    use = VALUES_AT[n]
                    act.wait_ge(ob_full, l * len(OB_USES) + OB_USES.index(use) + 1)
                    if use[1] == "D":
                        h = int(use[2])
                        act.activation(oB[:, h, :], OB[:, 0:T], ACT.Copy)
                        act.activation(oBq[:, h, :], OB[:, 0:T], ACT.Square).then_inc(ob_read, 1)
                    else:
                        p, r0 = int(use[2]), 0 if use[3] == "A" else 64
                        act.activation(oAH[r0:r0 + 64, p, :], OB[r0:r0 + 64, 0:T], ACT.Copy).then_inc(o_hi, 1)
                if n in TRANSPOSE_AT:
                    act.wait_ge(tr_full, l * len(TR_USES) + TR_USES.index(TRANSPOSE_AT[n]) + 1)
                    act.activation(PT[:, :], TR[:, 0:384], ACT.Copy).then_inc(tr_read, 1)
                if n in SCORES_AT:
                    exps(l, SCORES_AT[n])
                use = STATS_AT.get(n)
                if use == "LAT":
                    st_done(l, use)
                    act.activation(rdev[:, 0:T], ST[:, 0:T], ACT.Sqrt, bias=eps[:, :], scale=1.0 / QR)
                    act.activation(rdev[:, T:2 * T], ST[:, T:2 * T], ACT.Sqrt, bias=eps[:, :],
                                   scale=1.0 / KVR).then_inc(st_read, 1)
                elif use in ("SUB0", "SUB1"):
                    st_done(l, use)
                    act.activation(rdev[:, :], ST[:, :], ACT.Sqrt, bias=eps[:, :], scale=1.0 / P).then_inc(st_read, 1)
                elif use == "LNQ":
                    st_done(l, use)
                    act.activation(rdev[:, 0:T], ST[:, 0:T], ACT.Sqrt, bias=eps[:, :], scale=1.0 / CONV_CH).then_inc(st_read, 1)
                if n == 5:
                    act.wait_ge(lat_y, l + 1)
                    act.activation(latH[:, :, :].rearrange("p k t -> p (k t)"), lat[:, :, :].rearrange("p k t -> p (k t)"),
                                   ACT.Copy).then_inc(lat_hi, 1)
                if n in (18, 22):
                    i = (18, 22).index(n)
                    act.wait_ge(sub_y, l * 2 + i + 1)
                    act.activation(oBH[:, 2 * i:2 * i + 2, :].rearrange("p k t -> p (k t)"),
                                   oBq[:, 2 * i:2 * i + 2, :].rearrange("p k t -> p (k t)"), ACT.Copy).then_inc(sub_hi, 1)
                if n == 25:
                    act.wait_ge(cen_ready, l + 1)
                    act.activation(latq[:, 0:CT, :].rearrange("p k t -> p (k t)"), cv[:, :, :].rearrange("p k t -> p (k t)"),
                                   ACT.Square).then_inc(cen_sq, 1)
                if n == 28:
                    act.wait_ge(ln_y, l + 1)
                    for t in range(CT):
                        act.activation(cv[:, t, :], latq[:, t, :], ACT.Identity, bias=vec[:, V_LNB + t:V_LNB + t + 1])
                        ins = act.activation(ln_th[:, t, :], latq[:, t, :], ACT.Tanh, bias=half_b[:, t:t + 1],
                                             scale=0.5)
                    ins.then_inc(ln_t, 1)
                if n == 30:
                    act.wait_ge(ln_u, l + 1)
                    act.activation(uH[:, :, :].rearrange("p k t -> p (k t)"), latq[:, 0:CT, :].rearrange("p k t -> p (k t)"),
                                   ACT.Copy, scale=0.5).then_inc(ln_hi, 1)

            def up_step(l, n, r=0):
                i, b = divmod(n - UP, 2)
                high(l, n + 2, r)
                if b == 1:
                    act.wait_ge(pb_read[0], FREE + l * (PB_USES // 2) + (PB_UP + n - UP) // 2 + 1 + 2 * r)
                    act.activation(th[:, :, :].rearrange("p k t -> p (k t)"), ca[:, :, :].rearrange("p k t -> p (k t)"),
                                   ACT.Tanh, scale=0.5).then_inc(th_ready, 1)
                pb = full(l, PB_UP + n - UP, r)
                dst = (ca, cb)[b]
                act.wait_ge(gy_ready, FREE + l * (FT // 2) + i + 2 * r)
                for t in range(2):
                    col = b * FT + 2 * i + t
                    ins = act.activation(dst[:, t, :], pb[:, t * T:(t + 1) * T], ACT.Identity,
                                         bias=vec[:, bass.ds(V_FB + col + 4 * r, 1)],
                                         scale=vec[:, bass.ds(V_FW + 2 * 2 * FT + col + 4 * r, 1)])
                ins.then_inc(tap_ready, 1)
                if b == 1:
                    act.wait_ge(gy_ready, FREE + l * (FT // 2) + i + 1 + 2 * r)
                    act.activation(gH[:, bass.ds(2 * i + 4 * r, 2), :].rearrange("p k t -> p (k t)"),
                                   gy[:, :, :].rearrange("p k t -> p (k t)"), ACT.Copy).then_inc(g_hi, 1)

            with act.Fori(0, LAYERS) as l:
                high(l, 0)
                high(l, 1)
                norm(l, 0)
                for n in range(WO):
                    mixer_step(l, n)
                    if n >= WO - 2:
                        for u in range(2):
                            i = 2 * (n - (WO - 2)) + u
                            act.wait_ge(m_ready, l * 4 + i + 1)
                            act.activation(hH[:, 2 * i:2 * i + 2, :].rearrange("p k t -> p (k t)"),
                                           buf[:, 2 * i:2 * i + 2, :].rearrange("p k t -> p (k t)"), ACT.Copy,
                                           scale=0.5).then_inc(m_hi, 1)
                for n in range(WO, UP):
                    high(l, n + 2)
                norm(l, 1)
                with act.Fori(0, UP_LOOPS) as r:
                    for j in range(4):
                        up_step(l, UP + j, r)
                for n in range(UP + 4 * UP_LOOPS, DOWN):
                    up_step(l, n)
                for n in range(DOWN, CHUNKS - 2):
                    high(l, n + 2)

            for k in range(DT):
                act.wait_ge(x_ready, LAYERS * DT + k + 1)
                act.activation(buf[:, k, :], xT[:, k, :], ACT.Square).then_inc(sq_ready, 1)
            act.wait_ge(st_full, LAYERS * len(ST_USES) + 1)
            act.activation(rdev[:, 0:T], ST[:, 0:T], ACT.Sqrt, bias=eps[:, :], scale=1.0 / D).then_inc(st_read, 1)
            for a in range(2):
                act.wait_ge(out_turned, 2 * a + 2)
                act.activation(xn[:, 4 * a + 2:4 * a + 4, :].rearrange("p k t -> p (k t)"), OUT[a][1][:, :],
                               ACT.Copy).then_inc(out_ready[a], 1)

        @block.vector
        def _(dve):
            chain = Chain(dve, v_link)
            link = chain.link

            dve.memset(ones[:, :], 1.0)
            dve.memset(eps[:, :], EPS).then_inc(s_const, 1)
            dve.wait_ge(s_cst, 32)
            dve.tensor_copy(maskb[:, :], mask[:, :])
            dve.tensor_copy(identb[:, :], ident).then_inc(s_const, 1)
            dve.wait_ge(s_vtr, 1)
            dve.tensor_copy(c_act[:, 0, :], MI[:, 0:DT])
            dve.tensor_copy(fin_g[:, :], MI[:, DT:2 * DT]).then_inc(s_vt, 1)
            dve.wait_ge(s_cth, 1)
            dve.wait_ge(s_vt, 1)
            link(dve.scalar_tensor_tensor(c_act[:, 2, :], c_act[:, 1, :], 1.0, c_act[:, 0, :], ALU.add, ALU.mult))
            dve.tensor_scalar_mul(c_act[:, 2, :], c_act[:, 2, :], 0.5).then_inc(s_silu, 1)
            for b in range(4):
                dve.wait_ge(s_xtr, b + 1)
                dve.tensor_copy(xT[:, 2 * b:2 * b + 2, :].rearrange("p k t -> p (k t)"), DN[b][:, :]).then_inc(x_ready, 2)
            dve.wait_ge(s_lam, 16)
            for l in range(LAYERS):
                ins = dve.tensor_tensor(lam_p[:, l, :, :], lam_in[:, l, 0::2, :], lam_in[:, l, 1::2, :], ALU.mult)
            link(ins)
            dve.tensor_reduce(lam_s[:, :, :], lam_p[:, :, :, :], AX.X, ALU.add).then_inc(s_lame, 1)
            dve.wait_ge(s_pos, 16)
            link(dve.tensor_copy(turns[:, 0, :], pos_i[:, :]))
            dve.tensor_scalar(ang[:, 1, :], turns[:, 0, :], cst[:, C_INV + 1:C_INV + 2], None, ALU.mult)
            link(dve.tensor_scalar(ang[:, 0, :], turns[:, 0, :], cst[:, C_INV:C_INV + 1], None, ALU.mult))
            link(dve.tensor_scalar(turns[:, :, :], ang[:, :, :], 1.0 / (2 * math.pi), ROUND, ALU.mult, ALU.add))
            link(dve.tensor_scalar(turns[:, :, :], turns[:, :, :], ROUND, None, ALU.subtract))
            for part in (TWO_PI_1, TWO_PI_2, TWO_PI_3):
                link(dve.scalar_tensor_tensor(ang[:, :, :], turns[:, :, :], -part, ang[:, :, :], ALU.mult, ALU.add))
            edge = float(np.nextafter(np.float32(math.pi), np.float32(0)))
            link(dve.tensor_scalar(ang[:, :, :], ang[:, :, :], edge, -edge, ALU.min, ALU.max))
            link(dve.tensor_scalar(turns[:, :, :], ang[:, :, :], -1.0, None, ALU.mult))
            link(dve.tensor_tensor(turns[:, :, :], turns[:, :, :], ang[:, :, :], ALU.min))
            dve.tensor_scalar(turns[:, :, :], turns[:, :, :], math.pi / 2, None, ALU.add).then_inc(s_ang, 1)

            def ada_end(part, order, source):
                dve.wait_ge(mi_full, order)
                dve.tensor_tensor(mod[:, part * DT:(part + 1) * DT], MI[:, 0:DT],
                                  source[:, V_ADAB + part * DT:V_ADAB + (part + 1) * DT], ALU.add).then_inc(mi_read, 1)

            def ada_products(src, factor, halves, first):
                if first:
                    ins = dve.tensor_scalar(acc[:, :], src[:, 0, :], factor[:, 0:1], None, ALU.mult)
                else:
                    ins = dve.scalar_tensor_tensor(acc[:, :], src[:, 0, :], factor[:, 0:1], acc[:, :], ALU.mult, ALU.add)
                ins.then_inc(ada_half, 1)
                dve.wait_ge(ada_half, halves)
                dve.scalar_tensor_tensor(acc[:, :], src[:, 1, :], factor[:, 1:2], acc[:, :], ALU.mult,
                                         ALU.add).then_inc(ada_used, 1)

            def ada_step(l, a, r=0):
                serial = ADA_FIRST + l * ADA_CHUNKS + a + r
                dve.wait_ge(ada_in, (l * ADA_CHUNKS + a + 1) * 16 + 16 * r)
                if a == ADA_LOOP:
                    dve.wait_ge(acc_clear, l + 1)
                elif a % ADA_PART == 0:
                    dve.wait_ge(mi_full, 2 + l * 6 + a // ADA_PART)
                dve.wait_ge(ada_used, serial)
                factor = c_act[:, 2, bass.ds(2 * r, 2)] if a == ADA_LOOP else factors(a % ADA_PART)
                ada_products(ada, factor, serial + 1, a % ADA_PART == 0 and a != ADA_LOOP)

            dve.wait_ge(s_silu, 1)
            for a in range(ADA_FIRST):
                dve.wait_ge(ada_pre_in[a], 16)
                if a == ADA_PART:
                    ada_end(0, 1, vec_all[:, 0, :])
                if a:
                    dve.wait_ge(ada_used, a)
                ada_products(ada_pre[:, a, :, :], factors(a % ADA_PART), a + 1, a % ADA_PART == 0)
                if a == 2:
                    for l in range(LAYERS):
                        dve.wait_ge(s_vtr, 2 + l)
                        for at, count, b in ((0, ROWS_A, 0), (V_CW, ROWS_B, P), (V_FW, 4 * FT, 2 * P),
                                             (V_FW + 4 * FT, 2 * FT, 3 * P)):
                            dve.tensor_copy(vec_all[:, l, at:at + count], PB[l][:, b:b + count])
                        dve.tensor_copy(vec_all[:, l, V_LAM:V_LAM + 2],
                                        cst[:, C_LAM + 2 * l:C_LAM + 2 * l + 2]).then_inc(s_vt, 1)
                    dve.wait_ge(s_lamx, 1)
                    dve.wait_ge(s_vt, 1 + LAYERS)
                    link(dve.tensor_tensor(lamb[:, 0, :], lam_s[:, :, 1], lam_s[:, :, 0], ALU.subtract))
                    link(dve.tensor_tensor(lamb[:, 1, :], lamb[:, 0, :], vec_all[:, :, V_LAM], ALU.subtract))
            ada_end(1, 2, vec_all[:, 0, :])

            def low(l, n, r=0):
                s, cut = n % RAW, vector_share(n)
                dve.wait_ge(w_hi, l * CHUNKS + n + 1 + 4 * r)
                dve.tensor_tensor(wL[s][:, 0:cut], raw[s][:, 0:cut], wH[s][:, 0:cut].bitcast(F32),
                                  ALU.subtract).then_inc(w_lo[s], 1)

            def flat(t):
                return t.rearrange("p k t -> p (k t)")

            def norm(l, which):
                dve.wait_ge(st_read, FREE + l * len(ST_USES) + (1, 7)[which])
                link(dve.reciprocal(rdev[:, 0:T], rdev[:, 0:T]))
                for k in range(DT + 2):
                    if k < DT:
                        dve.scalar_tensor_tensor(xn[:, k, :], xT[:, k, :], gs[:, which, k:k + 1], rdev[:, 0:T], ALU.mult,
                                                 ALU.mult).then_inc(xn_ready, 1)
                    if k >= 2:
                        j = k - 2
                        dve.wait_ge(h_hi, l * 2 * DT + which * DT + j + 1)
                        dve.scalar_tensor_tensor(hL[:, j, :], xn[:, j, :], mod[:, 3 * which * DT + j:3 * which * DT + j + 1],
                                                 hH[:, j, :].bitcast(F32), ALU.add, ALU.subtract).then_inc(h_lo, 1)

            def rope(l, use):
                i = int(use[2]) if use[1] != "k" or use[2] != "r" else 0
                if use == "Rkr":
                    src, n0, n1, which, u = krope, 64, 96, 1, 3
                elif use[1] == "M":
                    src, n0, n1, which, u = qraw, 0, 96, 1, PB_MLA + 5 * i
                else:
                    src, n0, n1, which, u = (qraw, kraw)[use[1] == "k"], 0, P, 0, PB_DIFF + 4 * i + (use[1] == "k")
                dve.wait_ge(pb_read[u % 2], FREE + l * (PB_USES // 2) + u // 2 + 1)
                turned = l * len(TR_USES) + TR_USES.index(use) + 1
                if use == "Rkr":
                    dve.tensor_tensor(kM[64:96, 0, :], krope[64:96, :], cos[64:96, 1, :], ALU.mult)
                    dve.wait_ge(tr_full, turned)
                    dve.tensor_tensor(rot_s[64:96, 0, :], TR[64:96, 0:T], sin[64:96, 1, :], ALU.mult).then_inc(tr_read, 1)
                    dve.wait_ge(tr_read, FREE + turned)
                    link(dve.tensor_tensor(kM[64:96, 0, :], kM[64:96, 0, :], rot_s[64:96, 0, :], ALU.add))
                    link(dve.tensor_copy(kM[64:96, 1, :], kM[64:96, 0, :]))
                    return
                dst = {"q": qD, "k": kD, "M": qM}[use[1]][n0:n1, :, :]
                c, s = (t[n0:n1, which, :].unsqueeze(1).broadcast_to([n1 - n0, 2, T]) for t in (cos, sin))
                dve.wait_ge(tr_full, turned)
                dve.tensor_tensor(dst, src[n0:n1, :, :], c, ALU.mult)
                dve.tensor_tensor(rot_s[n0:n1, :, :], TR[n0:n1, :].rearrange("p (k t) -> p k t", k=2), s,
                                  ALU.mult).then_inc(tr_read, 1)
                dve.wait_ge(tr_read, FREE + turned)
                dve.tensor_tensor(dst, dst, rot_s[n0:n1, :, :], ALU.add).then_inc(roped, 1)
                dve.wait_ge(roped, l * 8 + ROPED.index(use) + 1)

            def row_max(l, use):
                dve.wait_ge(sc_full, l * len(SC_USES) + SC_USES.index(use) + 1)
                for m in range(2):
                    for b, (lo, hi) in enumerate(((0, 128), (128, 384))):
                        i = 2 * m + b
                        ins = dve.tensor_reduce(nmax[:, i:i + 1], SC[m][:, lo:hi], AX.X, ALU.max, negate=True)
                link(ins)
                dve.tensor_scalar_mul(nb[:, :], nmax[:, :], SCALE_D if use[0] == "D" else SCALE_M).then_inc(nb_ready, 1)

            def weights(l, use):
                dve.wait_ge(e_ready, FREE + l * len(SC_USES) + SC_USES.index(use) + 1)
                before = {"D0": None, "M0": "TD3"}.get(use, f"TD{int(use[1]) - 1}" if use[0] == "D" else f"TM{int(use[1]) - 1}B")
                if before:
                    dve.wait_ge(tr_full, l * len(TR_USES) + TR_USES.index(before) + 1)
                link(dve.reciprocal(rsum[:, :], esum[:, :]))
                if use[0] == "D":
                    link(dve.tensor_scalar(rsum[:, 2:4], rsum[:, 2:4], lam_now[:, :], None, ALU.mult))
                    dve.tensor_scalar(W[:, 0, 0:128], E[:, 0, 0:128], rsum[:, 0:1], None, ALU.mult)
                    link(dve.tensor_scalar(W[:, 0, 128:384], E[:, 0, 128:384], rsum[:, 1:2], None, ALU.mult))
                    dve.scalar_tensor_tensor(W[:, 0, 0:128], E[:, 1, 0:128], rsum[:, 2:3], W[:, 0, 0:128], ALU.mult, ALU.add)
                    ins = dve.scalar_tensor_tensor(W[:, 0, 128:384], E[:, 1, 128:384], rsum[:, 3:4], W[:, 0, 128:384],
                                                   ALU.mult, ALU.add)
                else:
                    for m in range(2):
                        dve.tensor_scalar(W[:, m, 0:128], E[:, m, 0:128], rsum[:, 2 * m:2 * m + 1], None, ALU.mult)
                        ins = dve.tensor_scalar(W[:, m, 128:384], E[:, m, 128:384], rsum[:, 2 * m + 1:2 * m + 2], None, ALU.mult)
                ins.then_inc(w_ready, 1)

            def taps(pair, k0, k1):
                for k in range(TAPS - 1 - k0, TAPS - 1 - k1, -1):
                    for t in (2 * pair, 2 * pair + 1):
                        ins = dve.scalar_tensor_tensor(cv[:, t, :], up_pad[:, t, k:k + T],
                                                       vec[:, V_CW + k * CT + t:V_CW + k * CT + t + 1], cv[:, t, :],
                                                       ALU.mult, ALU.add)
                    if (pair, k) == (1, 0):
                        ins.then_inc(conv_done, 1)
                    else:
                        link(ins)

            def mixer_step(l, n):
                if n - 1 in SCORES_AT:
                    weights(l, SCORES_AT[n - 1])
                low(l, n + 2)
                if n in (DIFF + 4, DIFF + 9):
                    i = (n - DIFF) // 5
                    u = PB_DIFF + 4 * i + 3
                    dve.wait_ge(pb_read[0], FREE + l * (PB_USES // 2) + (u - 1) // 2 + 1)
                    dve.wait_ge(pb_full, l * PB_USES + u + 1)
                    dve.scalar_tensor_tensor(up_pad[:, 2 * i:2 * i + 2, TAPS - 1:], cth[:, :, :], 1.0,
                                             PB[1][:, :].rearrange("p (k t) -> p k t", k=2), ALU.add,
                                             ALU.mult).then_inc(pb_read[1], 1)
                    dve.wait_ge(pb_read[1], FREE + l * (PB_USES // 2) + u // 2 + 1)
                    for t in (2 * i, 2 * i + 1):
                        ins = dve.tensor_scalar(cv[:, t, :], up_pad[:, t, TAPS - 1:],
                                                vec[:, V_CW + (TAPS - 1) * CT + t:V_CW + (TAPS - 1) * CT + t + 1],
                                                vec[:, V_CB + t:V_CB + t + 1], ALU.mult, ALU.add)
                    link(ins)
                if n in VALUES_AT and VALUES_AT[n][1] == "M":
                    use = VALUES_AT[n]
                    p, r0 = int(use[2]), 0 if use[3] == "A" else 64
                    dve.wait_ge(o_hi, l * 8 + 2 * p + (use[3] == "B") + 1)
                    dve.tensor_tensor(oAL[r0:r0 + 64, p, :], OB[r0:r0 + 64, 0:T], oAH[r0:r0 + 64, p, :].bitcast(F32),
                                      ALU.subtract).then_inc(ob_read, 1)
                for use in ROTATE_AT.get(n, ()):
                    rope(l, use)
                if n in SCORES_AT:
                    row_max(l, SCORES_AT[n])
                if n == 4:
                    dve.wait_ge(st_read, FREE + l * len(ST_USES) + 2)
                    link(dve.reciprocal(rdev[:, :], rdev[:, :]))
                    for k in range(QT + KVT):
                        g, part = (V_QG + k, 0) if k < QT else (V_KVG + k - QT, T)
                        ins = dve.scalar_tensor_tensor(lat[:, k, :], lat[:, k, :], vec[:, g:g + 1], rdev[:, part:part + T],
                                                       ALU.mult, ALU.mult)
                    ins.then_inc(lat_y, 1)
                if n == 5:
                    dve.memset(up_pad[:, :, 0:TAPS - 1], 0.0)
                if n == 6:
                    dve.wait_ge(lat_hi, l + 1)
                    dve.tensor_tensor(flat(latL[:, :, :]), flat(lat[:, :, :]), flat(latH[:, :, :]).bitcast(F32),
                                      ALU.subtract).then_inc(lat_lo, 1)
                if n in (18, 21):
                    i = (18, 21).index(n)
                    dve.wait_ge(st_read, FREE + l * len(ST_USES) + 3 + i)
                    link(dve.reciprocal(rdev[:, :], rdev[:, :]))
                    dve.scalar_tensor_tensor(flat(oBq[:, 2 * i:2 * i + 2, :]), flat(oB[:, 2 * i:2 * i + 2, :]), sub_g[:, :],
                                             rdev[:, :], ALU.mult, ALU.mult).then_inc(sub_y, 1)
                if n in (19, 23):
                    i = (19, 23).index(n)
                    dve.wait_ge(sub_hi, l * 2 + i + 1)
                    dve.tensor_tensor(flat(oBL[:, 2 * i:2 * i + 2, :]), flat(oBq[:, 2 * i:2 * i + 2, :]),
                                      flat(oBH[:, 2 * i:2 * i + 2, :]).bitcast(F32), ALU.subtract).then_inc(sub_lo, 1)
                if n in TAPS_AT:
                    taps(*TAPS_AT[n])
                if n == 24:
                    dve.wait_ge(st_full, l * len(ST_USES) + 5)
                    dve.tensor_scalar(rdev[:, 0:T], ST[:, 0:T], -1.0 / CONV_CH, None, ALU.mult).then_inc(st_read, 1)
                    dve.wait_ge(st_read, FREE + l * len(ST_USES) + 5)
                    dve.wait_ge(conv_done, l + 1)
                    for k in range(0, CT, 2):
                        ins = dve.tensor_tensor(cv[:, k:k + 2, :], cv[:, k:k + 2, :],
                                                rdev[:, 0:T].unsqueeze(1).broadcast_to([P, 2, T]), ALU.add)
                    ins.then_inc(cen_ready, 1)
                if n == 27:
                    dve.wait_ge(st_read, FREE + l * len(ST_USES) + 6)
                    link(dve.reciprocal(rdev[:, 0:T], rdev[:, 0:T]))
                    for t in range(CT):
                        ins = dve.scalar_tensor_tensor(latq[:, t, :], cv[:, t, :], vec[:, V_LNG + t:V_LNG + t + 1],
                                                       rdev[:, 0:T], ALU.mult, ALU.mult)
                    ins.then_inc(ln_y, 1)
                if n == 29:
                    dve.wait_ge(ln_t, l + 1)
                    dve.scalar_tensor_tensor(flat(latq[:, 0:CT, :]), flat(ln_th), 1.0, flat(cv[:, :, :]), ALU.add,
                                             ALU.mult).then_inc(ln_u, 1)
                if n == 31:
                    dve.wait_ge(ln_hi, l + 1)
                    dve.scalar_tensor_tensor(flat(uL[:, :, :]), flat(latq[:, 0:CT, :]), 0.5, flat(uH[:, :, :]).bitcast(F32),
                                             ALU.mult, ALU.subtract).then_inc(ln_lo, 1)
                if n >= OUTS:
                    b, half = divmod(n - OUTS, 2)
                    for u in range(2):
                        i = 2 * half + u
                        use = PB_OUTS + 2 * (n - OUTS) + u
                        dve.wait_ge(pb_full, l * PB_USES + use + 1)
                        g = flat(G[:, (2 - b) * DT + 2 * i:(2 - b) * DT + 2 * i + 2, :])
                        dst = flat(buf[:, 2 * i:2 * i + 2, :])
                        to = dst if b == 0 else flat(xn[:, 2 * i:2 * i + 2, :])
                        dve.scalar_tensor_tensor(to, g, 1.0, PB[use % 2][:, :], ALU.add, ALU.mult).then_inc(pb_read[use % 2], 1)
                        if b:
                            dve.wait_ge(pb_read[use % 2], FREE + l * (PB_USES // 2) + use // 2 + 1)
                            ins = dve.tensor_tensor(dst, dst, to, ALU.add)
                            if b == 2:
                                ins.then_inc(m_ready, 1)
                            else:
                                link(ins)
                if n >= WO - 2:
                    for i in range(2 * (n - WO + 2), 2 * (n - WO + 2) + 2):
                        dve.wait_ge(m_hi, l * 4 + i + 1)
                        dve.scalar_tensor_tensor(flat(hL[:, 2 * i:2 * i + 2, :]), flat(buf[:, 2 * i:2 * i + 2, :]), 0.5,
                                                 flat(hH[:, 2 * i:2 * i + 2, :]).bitcast(F32), ALU.mult,
                                                 ALU.subtract).then_inc(m_lo, 1)
                ada_work(l, n)

            def ada_work(l, n):
                if n in ADA_STEPS:
                    a = ADA_STEPS.index(n)
                    if a < ADA_NEXT:
                        ada_step(l, a)
                    else:
                        with dve.If(l < LAYERS - 1):
                            ada_step(l, a)
                for at, q in ADA_REDUCE_AT.items():
                    if at + 1 == n and ADA_PARTS[q] < 2:
                        with dve.If(l < LAYERS - 1):
                            ada_end(ADA_PARTS[q], l * 6 + 3 + q, vec_all[:, LAYERS - 1, :])
                    elif at + 1 == n:
                        ada_end(ADA_PARTS[q], l * 6 + 3 + q, vec)
                        if q == 2:
                            dve.wait_ge(mi_read, l * 6 + 3 + q)
                            link(dve.scalar_tensor_tensor(gs[:, 1, :], mod[:, 4 * DT:5 * DT], 1.0, vec[:, V_N2:V_N2 + DT],
                                                          ALU.add, ALU.mult))

            def up_step(l, n, r=0):
                i, b = divmod(n - UP, 2)
                u = PB_UP + n - UP
                pb, dst = PB[u % 2], (ca, cb)[b]
                tap = lambda k, t: vec[:, bass.ds(V_FW + k * 2 * FT + b * FT + 2 * i + t + 4 * r, 1)]
                low(l, n + 2, r)
                if b == 1:
                    dve.wait_ge(th_ready, l * (FT // 2) + i + 1 + 2 * r)
                    link(dve.scalar_tensor_tensor(flat(gy[:, :, :]), flat(th[:, :, :]), 1.0, flat(ca[:, :, :]), ALU.add, ALU.mult))
                dve.wait_ge(tap_ready, l * 22 + n - UP + 1 + 4 * r)
                for k in (1, 0):
                    lag = FTAPS - 1 - k
                    for t in range(2):
                        ins = dve.scalar_tensor_tensor(dst[:, t, lag:], pb[:, t * T:(t + 1) * T - lag], tap(k, t), dst[:, t, lag:],
                                                       ALU.mult, ALU.add)
                    if k == 1:
                        link(ins)
                ins.then_inc(pb_read[u % 2], 1)
                dve.wait_ge(pb_read[u % 2], FREE + l * (PB_USES // 2) + u // 2 + 1 + 2 * r)
                if b == 1:
                    dve.scalar_tensor_tensor(flat(gy[:, :, :]), flat(gy[:, :, :]), 0.5, flat(cb[:, :, :]), ALU.mult,
                                             ALU.mult).then_inc(gy_ready, 1)
                    dve.wait_ge(g_hi, l * (FT // 2) + i + 1 + 2 * r)
                    dve.tensor_tensor(flat(gL[:, bass.ds(2 * i + 4 * r, 2), :]), flat(gy[:, :, :]),
                                      flat(gH[:, bass.ds(2 * i + 4 * r, 2), :]).bitcast(F32), ALU.subtract).then_inc(g_lo, 1)

            def flush_vectors(l):
                link(dve.tensor_copy(vec[:, :], vec_all[:, l, :]))
                dve.tensor_scalar_mul(vec[:, V_CW:V_CW + ROWS_B], vec[:, V_CW:V_CW + ROWS_B], 0.5)
                dve.tensor_scalar_mul(half_b[:, :], vec[:, V_LNB:V_LNB + CT], 0.5)
                dve.tensor_scalar(sub_g[:, :], vec[:, V_SUB:V_SUB + 1], vec[:, V_LAM + 1:V_LAM + 2], None, ALU.mult)
                dve.tensor_copy(lam_now[:, :], lamb[:, 1, bass.ds(l, 1)])
                dve.wait_ge(mi_read, l * 6 + 2)
                link(dve.scalar_tensor_tensor(gs[:, 0, :], mod[:, DT:2 * DT], 1.0, vec[:, V_N1:V_N1 + DT], ALU.add, ALU.mult))

            before_loop = chain.n
            chain.n = 0
            with dve.Fori(0, LAYERS) as l:
                chain.base = l * V_LINKS + before_loop
                flush_vectors(l)
                low(l, 0)
                low(l, 1)
                norm(l, 0)
                for n in range(WO):
                    mixer_step(l, n)
                for n in range(WO, UP):
                    low(l, n + 2)
                    u = PB_WO + n - WO
                    dve.wait_ge(pb_full, l * PB_USES + u + 1)
                    for t in range(2):
                        k = 2 * (n - WO) + t
                        ins = dve.scalar_tensor_tensor(xT[:, k, :], PB[u % 2][:, t * T:(t + 1) * T],
                                                       mod[:, 2 * DT + k:2 * DT + k + 1], xT[:, k, :], ALU.mult, ALU.add)
                    ins.then_inc(pb_read[u % 2], 1)
                    ada_work(l, n)
                norm(l, 1)
                dve.wait_ge(mi_full, 2 + l * 6 + ADA_LOOP // ADA_PART)
                dve.memset(acc[:, :], 0.0).then_inc(acc_clear, 1)
                ahead = chain.n
                chain.n = 0
                with dve.Fori(0, UP_LOOPS) as r:
                    chain.base = l * V_LINKS + before_loop + ahead + r * V_LINKS_UP
                    for j in range(4):
                        up_step(l, UP + j, r)
                        if j == 2:
                            ada_step(l, ADA_LOOP, r)
                assert chain.n == V_LINKS_UP, chain.n
                chain.n = ahead + UP_LOOPS * V_LINKS_UP
                chain.base = l * V_LINKS + before_loop
                for n in range(UP + 4 * UP_LOOPS, DOWN):
                    up_step(l, n)
                    ada_work(l, n)
                for n in range(DOWN, CHUNKS):
                    if n + 2 < CHUNKS:
                        low(l, n + 2)
                    ada_work(l, n)
                dve.wait_ge(mi_read, l * 6 + 6)
                for k in range(DT):
                    if k == DT - 2:
                        dve.wait_ge(down_used, RAW + (l + 1) * (FT // 2))
                    elif k % 2 == 0:
                        dve.wait_ge(down_done, l * 3 + k // 2 + 1)
                    dve.scalar_tensor_tensor(xT[:, k, :], DN[k // 2][:, (k % 2) * T:(k % 2 + 1) * T],
                                             mod[:, 5 * DT + k:5 * DT + k + 1], xT[:, k, :], ALU.mult,
                                             ALU.add).then_inc(x_ready, 1)
                ada_work(l, CHUNKS)
                assert chain.n == V_LINKS, chain.n

            chain.base, chain.n = LAYERS * V_LINKS + before_loop, 0
            dve.wait_ge(st_read, FREE + LAYERS * len(ST_USES) + 1)
            link(dve.reciprocal(rdev[:, 0:T], rdev[:, 0:T]))
            for k in range(DT):
                dve.scalar_tensor_tensor(buf[:, k, :], xT[:, k, :], fin_g[:, k:k + 1], rdev[:, 0:T], ALU.mult,
                                         ALU.mult).then_inc(fin_y, 1)
            for a in range(2):
                dve.wait_ge(out_turned, 2 * a + 1)
                dve.tensor_copy(flat(xn[:, 4 * a:4 * a + 2, :]), OUT[a][0][:, :]).then_inc(out_ready[a], 1)

        @block.tensor
        def _(pe):
            def after(s, count):
                pe.wait_ge(s, count)

            after(s_cst, 32)
            after(s_cvec, 32)
            pe.transpose(MI[:, 0:2 * DT], rows[0:2 * DT, 8, :], ident[0:2 * DT, 0:2 * DT]).then_inc(s_vtr, 1)
            after(s_x, 16)
            x_rows = xn[:, :, :].rearrange("p (a k) t -> p a (k t)", a=2)
            for b in range(4):
                for k in (2 * b, 2 * b + 1):
                    for a in range(2):
                        ins = pe.transpose(DN[b][:, (k % 2) * T + a * P:(k % 2) * T + (a + 1) * P],
                                           x_rows[:, a, k * P:(k + 1) * P], ident)
                ins.then_inc(s_xtr, 1)
            after(s_vec, 16 * VEC_LOADS)
            for l in range(LAYERS):
                for q, count in enumerate((ROWS_A, ROWS_B, 4 * FT, 2 * FT)):
                    ins = pe.transpose(PB[l][:, q * P:q * P + count], rows[0:count, 4 * l + q, :], ident[0:count, 0:count])
                ins.then_inc(s_vtr, 1)
            after(s_const, 1)
            after(s_vt, 1)

            def reduce_ada():
                for m in range(DT):
                    ins = pe.matmul(MI[:, m:m + 1], acc[:, m * P:(m + 1) * P], ones[:, 0:1], start=True, stop=True)
                ins.then_inc(mi_full, 1)

            for part in range(2):
                after(ada_used, ADA_PART * (part + 1))
                if part:
                    after(mi_read, part)
                reduce_ada()
            after(s_const, 2)

            def split_ready(l, n, r=0):
                after(w_lo[n % RAW], l * (CHUNKS // RAW) + n // RAW + 1 + r)
                after(w_lo_pool[n % RAW], l * (CHUNKS // RAW) + n // RAW + 1 + r)
                return wH[n % RAW], wL[n % RAW]

            def pb_free(l, u, r=0):
                after(pb_read[u % 2], FREE + l * (PB_USES // 2) + u // 2 + 2 * r)
                return PB[u % 2]

            def free(l, s, uses, use):
                after(s, FREE + l * len(uses) + uses.index(use))

            def blocks(out, wh, wl, at, m, kt, xh, xl, first=True, last=True, ready=None):
                for k in range(kt):
                    if ready is not None:
                        after(*ready(k))
                    a, b = at(wh, k), at(wl, k)
                    pe.matmul(out, a, xh(k), start=first and k == 0, stop=False, skip_group_check=True)
                    pe.matmul(out, a, xl(k), start=False, stop=False, skip_group_check=True)
                    ins = pe.matmul(out, b, xh(k), start=False, stop=last and k == kt - 1, skip_group_check=True)
                return ins

            def cols(width, c0, m):
                return lambda w, k: w[:, k * width + c0:k * width + c0 + m]

            def pair(pb, wh, wl, width, c0, kt, xh, xl, ready=None):
                for t in range(2):
                    ins = blocks(pb[:, t * T:(t + 1) * T], wh, wl, cols(width, c0 + t * P, P), P, kt, xh, xl,
                                 ready=ready if t == 0 else None)
                return ins

            hh, hl = (lambda k: hH[:, k, :]), (lambda k: hL[:, k, :])

            def statistic(l, use):
                if use == "LAT":
                    for u in range(3):
                        after(pb_read[u % 2], FREE + l * (PB_USES // 2) + u // 2 + 1)
                    sums = [(latq[:, 0:QT, :], QT, 0), (latq[:, QT:QT + KVT, :], KVT, T)]
                elif use in ("SUB0", "SUB1"):
                    i = int(use[3])
                    after(ob_read, FREE + l * len(OB_USES) + OB_USES.index(("PD1", "PD3")[i]) + 1)
                    sums = None
                elif use == "LNS":
                    after(conv_done, l + 1)
                    sums = [(cv[:, :, :], CT, 0)]
                else:
                    after(cen_sq, l + 1)
                    sums = [(latq[:, 0:CT, :], CT, 0)]
                free(l, st_read, ST_USES, use)
                if sums is None:
                    pe.matmul(ST[:, :], ones[:, :], oBq[:, 2 * i:2 * i + 2, :].rearrange("p k t -> p (k t)"), start=True,
                              stop=True).then_inc(st_full, 1)
                    return
                for src, kt, at in sums:
                    for k in range(kt):
                        ins = pe.matmul(ST[:, at:at + T], ones[:, :], src[:, k, :], start=(k == 0), stop=(k == kt - 1))
                ins.then_inc(st_full, 1)

            def norm_sum(l, which):
                free(l, st_read, ST_USES, ("N1", "N2")[which])
                for k in range(DT):
                    after(sq_ready, l * 2 * DT + which * DT + k + 1)
                    ins = pe.matmul(ST[:, 0:T], ones[:, :], buf[:, k, :], start=(k == 0), stop=(k == DT - 1))
                ins.then_inc(st_full, 1)

            def h_part(l, which):
                return lambda k: (h_lo, l * 2 * DT + which * DT + k + 1)

            def attention(l, n):
                if n in VALUES_AT:
                    use = VALUES_AT[n]
                    before = "T" + use[1:]
                    after(tr_read, FREE + l * len(TR_USES) + TR_USES.index(before) + 1)
                    free(l, ob_read, OB_USES, use)
                    if use[1] == "D":
                        i, h = divmod(int(use[2]), 2)
                        v = [vD[i][:, t, h * P:(h + 1) * P] for t in range(2)]
                    else:
                        v = [vM[int(use[2]) % 2][:, t, :] for t in range(2)]
                    pe.matmul(OB[:, 0:T], v[0], PT[:, 0:T], start=True, stop=False, skip_group_check=True)
                    pe.matmul(OB[:, P:T], v[1], PT[:, T:T + P], start=False, stop=True,
                              skip_group_check=True).then_inc(ob_full, 1)
                if n in TRANSPOSE_AT:
                    use = TRANSPOSE_AT[n]
                    m = 1 if use[1] == "M" and use[3] == "B" else 0
                    after(w_ready, l * len(SC_USES) + SC_USES.index(use[1:3]) + 1)
                    free(l, tr_read, TR_USES, use)
                    for b in range(3):
                        ins = pe.transpose(TR[:, b * P:(b + 1) * P], W[:, m, b * P:(b + 1) * P], ident)
                    ins.then_inc(tr_full, 1)
                for use in ROTATE_AT.get(n, ()):
                    free(l, tr_read, TR_USES, use)
                    if use == "Rkr":
                        after(pb_read[1], FREE + l * (PB_USES // 2) + 2)
                        ins = pe.matmul(TR[0:96, 0:T], cst[0:96, C_RM:C_RM + 96], krope[0:96, :], start=True, stop=True)
                    elif use[1] == "M":
                        u = PB_MLA + 5 * int(use[2])
                        after(pb_read[u % 2], FREE + l * (PB_USES // 2) + u // 2 + 1)
                        ins = pe.matmul(TR[0:96, :], cst[0:96, C_RM:C_RM + 96],
                                        qraw[0:96, :, :].rearrange("p k t -> p (k t)"), start=True, stop=True)
                    else:
                        u = PB_DIFF + 4 * int(use[2]) + (use[1] == "k")
                        after(pb_read[u % 2], FREE + l * (PB_USES // 2) + u // 2 + 1)
                        src = (qraw, kraw)[use[1] == "k"]
                        ins = pe.matmul(TR[:, :], cst[:, C_RD:C_RD + P], src[:, :, :].rearrange("p k t -> p (k t)"),
                                        start=True, stop=True)
                    ins.then_inc(tr_full, 1)
                if n in SCORES_AT:
                    use = SCORES_AT[n]
                    h = int(use[1])
                    after(roped, l * 8 + (2 * (h // 2 + 1) if use[0] == "D" else 4 + h + 1))
                    if use[0] == "M":
                        u = PB_MLA + 5 * h + 1
                        after(pb_read[u % 2], FREE + l * (PB_USES // 2) + u // 2 + 1)
                    free(l, e_ready, SC_USES, use)
                    for m in range(2):
                        if use[0] == "D":
                            q, k = (s[m * HD:(m + 1) * HD, h % 2, :] for s in (qD, kD))
                        else:
                            q, k = (s[0:96, m, :] for s in (qM, kM))
                        pe.matmul(SC[m][:, 0:384], identb[:, :], maskb[:, :], start=True, stop=False, skip_group_check=True)
                        pe.matmul(SC[m][:, 0:128], q[:, 0:P], k[:, 0:P], start=False, stop=False, skip_group_check=True)
                        ins = pe.matmul(SC[m][:, 128:384], q[:, P:T], k[:, :], start=False, stop=True, skip_group_check=True)
                    ins.then_inc(sc_full, 1)

            def reduce_ada_at(l, n):
                q = ADA_REDUCE_AT.get(n)
                if q is None:
                    return

                def go():
                    after(ada_used, ADA_FIRST + l * ADA_CHUNKS + ADA_PART * (q + 1))
                    after(mi_read, l * 6 + 2 + q)
                    reduce_ada()

                if ADA_PARTS[q] < 2:
                    with pe.If(l < LAYERS - 1):
                        go()
                else:
                    go()

            def chunk(l, n, r=0):
                wh, wl = split_ready(l, n, r)
                if n < LAT + 3:
                    pb = pb_free(l, n)
                    if n < 2:
                        ins = pair(pb, wh, wl, 256, 0, DT, hh, hl, ready=h_part(l, 0) if n == 0 else None)
                        ins.then_inc(pb_full, 1)
                    else:
                        blocks(pb[:, 0:T], wh, wl, cols(P + ROPE, 0, P), P, DT, hh, hl).then_inc(pb_full, 1)
                        pb = pb_free(l, 3)
                        blocks(pb[0:96, 0:T], wh, wl, cols(P + ROPE, P - NOPE, 96), 96, DT, hh, hl).then_inc(pb_full, 1)
                elif n < MLA:
                    i, what = divmod(n - DIFF, 5)
                    if what == 2:
                        free(l, ob_read, OB_USES, f"V{i}")
                        for t in range(2):
                            o = OB[:, t * 256:(t + 1) * 256]
                            for k in range(DT):
                                xh, xl = (x_[:, k, t * P:(t + 1) * P] for x_ in (hH, hL))
                                a, b = (w[:, k * 256:(k + 1) * 256] for w in (wh, wl))
                                pe.matmul(o, xh, a, start=(k == 0), stop=False)
                                pe.matmul(o, xl, a, start=False, stop=False)
                                ins = pe.matmul(o, xh, b, start=False, stop=(k == DT - 1))
                        ins.then_inc(ob_full, 1)
                    else:
                        u = PB_DIFF + 4 * i + (what if what < 2 else what - 1)
                        pair(pb_free(l, u), wh, wl, 256, 0, DT, hh, hl).then_inc(pb_full, 1)
                elif n < OUTS:
                    p, what = divmod(n - MLA, 5)
                    u = PB_MLA + 5 * p + what
                    lh, ll = (lambda k: latH[:, k, :]), (lambda k: latL[:, k, :])
                    if what == 0:
                        after(lat_lo, l + 1)
                        pb = pb_free(l, u)
                        for j in range(2):
                            ins = blocks(pb[0:96, j * T:(j + 1) * T], wh, wl, cols(192, 96 * j, 96), 96, QT, lh, ll)
                        ins.then_inc(pb_full, 1)
                    elif what == 1:
                        lh, ll = (lambda k: latH[:, QT + k, :]), (lambda k: latL[:, QT + k, :])
                        pair(pb_free(l, u), wh, wl, 256, 0, KVT, lh, ll).then_inc(pb_full, 1)
                        free(l, ob_read, OB_USES, f"VM{p}")
                        for t in range(2):
                            o = OB[:, t * P:(t + 1) * P].rearrange("p (h d) -> p h d", h=2)
                            for k in range(KVT):
                                xh, xl = (x_[:, QT + k, t * P:(t + 1) * P] for x_ in (latH, latL))
                                a, b = (w[:, k * 256:(k + 1) * 256].rearrange("p (h d) -> p h d", h=2)[:, :, NOPE:]
                                        for w in (wh, wl))
                                pe.matmul(o, xh, a, start=(k == 0), stop=False)
                                pe.matmul(o, xl, a, start=False, stop=False)
                                ins = pe.matmul(o, xh, b, start=False, stop=(k == KVT - 1))
                        ins.then_inc(ob_full, 1)
                    else:
                        pair(pb_free(l, u), wh, wl, 256, 0, DT, hh, hl).then_inc(pb_full, 1)
                elif n < WO:
                    b, half = divmod(n - OUTS, 2)
                    if b == 0:
                        after(ln_lo, l + 1)
                    elif b == 1:
                        after(sub_lo, 2 * l + 2)
                    else:
                        after(ob_read, FREE + (l + 1) * len(OB_USES))
                    oh, ol = ((uH, uL), (oBH, oBL), (oAH, oAL))[b]
                    for v in range(2):
                        u = PB_OUTS + 2 * (n - OUTS) + v
                        pair(pb_free(l, u), wh, wl, 512, 256 * v, 4, (lambda k: oh[:, k, :]),
                             (lambda k: ol[:, k, :])).then_inc(pb_full, 1)
                elif n < UP:
                    after(m_lo, l * 4 + 4)
                    pair(pb_free(l, PB_WO + n - WO), wh, wl, 256, 0, DT, hh, hl).then_inc(pb_full, 1)
                elif n < DOWN:
                    pair(pb_free(l, PB_UP + n - UP, r), wh, wl, 256, 0, DT, hh, hl,
                         ready=h_part(l, 1) if n == UP else None).then_inc(pb_full, 1)
                else:
                    i = n - DOWN
                    after(g_lo, l * (FT // 2) + i + 1)
                    for k in range(DT):
                        ins = blocks(DN[k // 2][:, (k % 2) * T:(k % 2 + 1) * T], wh, wl, cols(1024, k * P, P), P, 2,
                                     lambda j: gH[:, 2 * i + j, :], lambda j: gL[:, 2 * i + j, :],
                                     first=(i == 0 and k % 2 == 0), last=(n == CHUNKS - 1))
                        if n == CHUNKS - 1 and k in (1, 3, 5):
                            ins.then_inc(down_done, 1)
                    ins.then_inc(down_used, 1)

            with pe.Fori(0, LAYERS) as l:
                norm_sum(l, 0)
                for n in range(UP):
                    chunk(l, n)
                    attention(l, n)
                    if n in STATS_AT:
                        statistic(l, STATS_AT[n])
                    reduce_ada_at(l, n)
                    if n == UP - 1:
                        norm_sum(l, 1)
                with pe.Fori(0, UP_LOOPS) as r:
                    for j in range(4):
                        chunk(l, UP + j, r)
                for n in range(UP + 4 * UP_LOOPS, CHUNKS):
                    chunk(l, n)
                    reduce_ada_at(l, n)

            free(LAYERS, st_read, ST_USES, "N1")
            for k in range(DT):
                after(sq_ready, LAYERS * 2 * DT + k + 1)
                ins = pe.matmul(ST[:, 0:T], ones[:, :], buf[:, k, :], start=(k == 0), stop=(k == DT - 1))
            ins.then_inc(st_full, 1)
            after(fin_y, DT)
            for a in range(2):
                for b in range(2):
                    for k in range(4):
                        ins = pe.transpose(OUT[a][b][:, k * P:(k + 1) * P], buf[:, 4 * b + k, a * P:(a + 1) * P], ident)
                    ins.then_inc(out_turned, 1)


_INS = ["x", "c", "positions", "ada_w", "ada_b", "norm1_g", "w_in", "q_norm_g", "w_uq", "kv_norm_g", "w_ukv", "w_out_mla",
        "diff_lambda", "diff_subln_g", "w_out_diff", "conv_dw_w", "conv_dw_b", "conv_ln_g", "conv_ln_b", "w_out_conv",
        "w_o", "norm2_g", "w_up", "ffn_conv_w", "ffn_conv_b", "w_down", "final_g"]


def kernel(**inputs):
    import concourse.bacc as bacc
    from concourse.bass_utils import run_bass_kernel_spmd

    nc = bacc.Bacc("TRN2", target_bir_lowering=False, num_devices=1)
    arrays, args = {}, []
    for name in _INS + ["consts"]:
        a = constants() if name == "consts" else np.ascontiguousarray(inputs[name])
        arrays[f"in_{name}"] = a
        args.append(nc.dram_tensor(f"in_{name}", a.shape, mybir.dt.from_np(a.dtype), kind="ExternalInput").ap())
    out = nc.dram_tensor("out_0", (1, T, D), F32, kind="ExternalOutput").ap()
    trunk_kernel(nc, *args, out)
    r = run_bass_kernel_spmd(nc, [arrays], core_ids=[0])
    return r.results[0]["out_0"]
```

```python
import math
from contextlib import ExitStack

import concourse.bass as bass
import numpy as np
from concourse import mybir

F32 = mybir.dt.float32
F32R = mybir.dt.float32r
BF16 = mybir.dt.bfloat16
I32 = mybir.dt.int32
ALU = mybir.AluOpType
ACT = mybir.ActivationFunctionType
AX = mybir.AxisListType

P = 128
LAYERS, D, T = 2, 1024, 256
DT = D // P
HEADS_M, NOPE, ROPE, QR, KVR = 8, 64, 32, 384, 256
QT, KVT = QR // P, KVR // P
HEADS_D, HD = 4, 64
CONV_CH, TAPS = 512, 31
CT = CONV_CH // P
FF, FTAPS = 2816, 3
FT = FF // P
EPS = 1e-6
SCALE_M = 1.0 / math.sqrt(NOPE + ROPE)
SCALE_D = 1.0 / math.sqrt(HD)
MASKED = -1e30

COL_K_ROPE = QR + KVR
COL_DQ = COL_K_ROPE + ROPE
COL_DK = COL_DQ + 2 * HEADS_D * HD
COL_DV = COL_DK + 2 * HEADS_D * HD
COL_CONV_A = COL_DV + 2 * HEADS_D * HD
COL_CONV_G = COL_CONV_A + CONV_CH
COL_GATE = COL_CONV_G + CONV_CH

LAT = 0
DIFF = LAT + 3
MLA = DIFF + 5 * 2
OUTS = MLA + 5 * 4
WO = OUTS + 6
UP = WO + 4
DOWN = UP + 2 * FF // 256
CHUNKS = DOWN + FT // 2
RAW = 4
SHARE, SHARE_UP = 3, 4
SLOT = 2048
UP_LOOPS = 4
assert CHUNKS % RAW == 0 and LAYERS == 2

PB_DIFF, PB_MLA, PB_OUTS, PB_WO, PB_UP = 4, 12, 32, 44, 48
PB_USES = PB_UP + 22

TR_USES = ["Rq0", "Rk0", "Rkr", "TD0", "Rq1", "TD1", "Rk1", "TD2", "TD3", "RM0", "TM0A", "TM0B", "RM1",
           "TM1A", "TM1B", "RM2", "TM2A", "TM2B", "RM3", "TM3A", "TM3B"]
OB_USES = ["V0", "PD0", "V1", "PD1", "PD2", "VM0", "PD3", "PM0A", "VM1", "PM0B", "PM1A", "VM2", "PM1B", "PM2A",
           "VM3", "PM2B", "PM3A", "PM3B"]
ST_USES = ["N1", "LAT", "SUB0", "SUB1", "LNS", "LNQ", "N2"]
SC_USES = ["D0", "D1", "D2", "D3", "M0", "M1", "M2", "M3"]

ROPED = ["Rq0", "Rk0", "Rq1", "Rk1", "RM0", "RM1", "RM2", "RM3"]

SCORES_AT = {6: "D0", 8: "D1", 11: "D2", 13: "D3", 16: "M0", 21: "M1", 26: "M2", 31: "M3"}
TRANSPOSE_AT = {8: "TD0", 10: "TD1", 13: "TD2", 15: "TD3", 18: "TM0A", 19: "TM0B", 23: "TM1A", 24: "TM1B",
                28: "TM2A", 29: "TM2B", 33: "TM3A", 34: "TM3B"}
VALUES_AT = {9: "PD0", 11: "PD1", 14: "PD2", 16: "PD3", 19: "PM0A", 20: "PM0B", 24: "PM1A", 25: "PM1B",
             29: "PM2A", 30: "PM2B", 34: "PM3A", 35: "PM3B"}
ROTATE_AT = {4: ["Rq0"], 5: ["Rk0"], 7: ["Rkr"], 9: ["Rq1"], 10: ["Rk1"], 15: ["RM0"], 20: ["RM1"], 25: ["RM2"],
             30: ["RM3"]}
STATS_AT = {3: "LAT", 17: "SUB0", 22: "SUB1", 26: "LNS", 28: "LNQ"}
TAPS_AT = {8 + i + 9 * pair: (pair, 1 + 30 * i // 9, 1 + 30 * (i + 1) // 9) for pair in range(2) for i in range(9)}

ADA_PART = 4
ADA_PARTS = [2, 3, 4, 5, 0, 1]
ADA_STEPS = [1, 4, 7, 24, 26, 28, 30, 32, 34, 36, 38, 40] + [None] * 4 + [60, 62, 64, 66, 68, 70, 72, 74]
ADA_LOADS = [min(n + (1 if n < 24 else 2), CHUNKS - 1) if n else None for n in ADA_STEPS]
ADA_LOOP, ADA_NEXT = 12, 16
ADA_REDUCE_AT = {25: 0, 33: 1, 41: 2, UP + 4 * UP_LOOPS: 3, 67: 4, 75: 5}
ADA_CHUNKS = len(ADA_STEPS)
ADA_FIRST = 2 * ADA_PART
assert UP_LOOPS == ADA_PART and UP + 4 * UP_LOOPS == 59

V_N1, V_N2, V_ADAB, V_QG, V_KVG, V_CB, V_LNG, V_LNB, V_SUB, V_FB = 0, 8, 16, 64, 67, 69, 73, 77, 81, 82
ROWS_A = V_FB + 2 * FT
V_CW = ROWS_A
ROWS_B = TAPS * CT
V_FW = V_CW + ROWS_B
V_LAM = V_FW + FTAPS * 2 * FT
NV = V_LAM + 2
C_ID, C_RD, C_RM, C_INV, C_LAM = 0, 128, 256, 352, 354
C_MASK = C_LAM + 2 * LAYERS
NC_CONST = C_MASK + 384

TWO_PI_1, TWO_PI_2 = 6.28125, 0.0019350051879882812
TWO_PI_3 = 2 * math.pi - TWO_PI_1 - TWO_PI_2
ROUND = 1.5 * 2.0**23


def constants():
    c = np.zeros((P, NC_CONST), np.float32)
    c[:, C_ID:C_ID + P] = np.eye(P)
    for base in (0, HD):
        for i in range(HD // 2):
            c[base + i + HD // 2, C_RD + base + i] = -1.0
            c[base + i, C_RD + base + i + HD // 2] = 1.0
    for i in range(ROPE // 2):
        c[NOPE + i + ROPE // 2, C_RM + NOPE + i] = -1.0
        c[NOPE + i, C_RM + NOPE + i + ROPE // 2] = 1.0
    later = np.triu(np.full((P, P), MASKED, np.float32), 1)
    c[:, C_MASK:C_MASK + P] = later
    c[:, C_MASK + 2 * P:C_MASK + 3 * P] = later
    inv = lambda dim: 1.0 / (np.float32(10000.0) ** (np.arange(0, dim, 2, dtype=np.float32) / np.float32(dim)))
    c[:, C_INV] = np.tile(inv(HD), 4)
    c[NOPE:NOPE + ROPE, C_INV + 1] = np.tile(inv(ROPE), 2)
    for l in range(LAYERS):
        init = 0.8 - 0.6 * math.exp(-0.3 * l)
        c[:, C_LAM + 2 * l] = init
        c[:, C_LAM + 2 * l + 1] = 1.0 - init
    return c


V_LINKS, V_LINKS_UP = 245, 14
FREE = 1
VEC_LOADS = 13


def chunk_size(n):
    if n == LAT + 2:
        return DT * (P + ROPE)
    if MLA <= n < OUTS and (n - MLA) % 5 == 0:
        return QT * 192
    if MLA <= n < OUTS and (n - MLA) % 5 == 2:
        return KVT * 256
    return SLOT


def gate_of(n):
    p, r = divmod(n - MLA, 5)
    return 3 * p + (1, 3, 4).index(r) if MLA <= n < OUTS and r in (1, 3, 4) else None


def last_use(n):
    if n < MLA:
        if n < DIFF:
            return "pb", n + 1 + (n == LAT + 2)
        i, what = divmod(n - DIFF, 5)
        if what == 2:
            return "ob", OB_USES.index(f"V{i}") + 1
        return "pb", PB_DIFF + 4 * i + (what if what < 2 else what - 1) + 1
    if n < OUTS:
        p, what = divmod(n - MLA, 5)
        return ("ob", OB_USES.index(f"VM{p}") + 1) if what == 2 else ("pb", PB_MLA + 5 * p + what + 1)
    if n < WO:
        return "pb", PB_OUTS + 2 * (n - OUTS) + 2
    return "pb", PB_WO + n - WO + 1


class Chain:

    def __init__(self, eng, sem):
        self.eng, self.sem, self.n, self.base = eng, sem, 0, 0

    def link(self, ins, behind=0):
        ins.then_inc(self.sem, 1)
        self.n += 1
        self.eng.wait_ge(self.sem, self.base + self.n - behind)


def trunk_kernel(nc, x, c, positions, ada_w, ada_b, norm1_g, w_in, q_norm_g, w_uq, kv_norm_g, w_ukv, w_out_mla,
                 diff_lambda, diff_subln_g, w_out_diff, conv_dw_w, conv_dw_b, conv_ln_g, conv_ln_b, w_out_conv,
                 w_o, norm2_g, w_up, ffn_conv_w, ffn_conv_b, w_down, final_g, consts, out):
    stack = ExitStack()
    with stack:
        def sb(name, shape, dt=F32, where=stack):
            return where.enter_context(nc.sbuf_tensor(name, shape, dt))

        def bank(name):
            return stack.enter_context(nc.psum_tensor(name, [P, 512], F32))

        def sem(name):
            return stack.enter_context(nc.semaphore(name))

        xT = sb("xT", [P, DT, T])
        xn = sb("xn", [P, DT, T])
        buf = sb("buf", [P, DT, T])
        hH = sb("hH", [P, DT, T], F32R)
        hL = sb("hL", [P, DT, T], F32R)
        loaded = ExitStack()
        raw = [sb(f"raw{i}", [P, SLOT], F32, loaded) for i in range(RAW)]
        loaded.close()
        wL = [sb(f"wL{i}", [P, SLOT], F32R) for i in range(RAW)]
        wH = [sb(f"wH{i}", [P, SLOT], F32R) for i in range(RAW)]
        ada = sb("ada", [P, 2, 1024])
        acc = sb("acc", [P, 1024])
        acc_pre = ada[:, 0, :]
        cst = sb("cst", [P, C_MASK])
        maskb = sb("maskb", [P, 384], BF16)
        identb = sb("identb", [P, P], BF16)
        ones = sb("ones", [P, P])
        eps = sb("eps", [P, 1])
        half_pi = sb("half_pi", [P, 1])
        touch = sb("touch", [P, 1])
        vec_all = sb("vec_all", [P, LAYERS, NV])
        vec = sb("vec", [P, NV])
        fin_g = sb("fin_g", [P, DT])
        c_act = sb("c_act", [P, 3, DT])
        mod = sb("mod", [P, 6 * DT])
        gs = sb("gs", [P, 2, DT])
        lamb = sb("lamb", [P, 2, LAYERS])
        sub_g = sb("sub_g", [P, 1])
        lam_now = sb("lam_now", [P, 1])
        half_b = sb("half_b", [P, CT])
        cos = sb("cos", [P, 2, T])
        sin = sb("sin", [P, 2, T])
        rdev = sb("rdev", [P, 512])
        ident = cst[:, C_ID:C_ID + P]

        first = ExitStack()
        rows = sb("rows", [P, 9, P], F32, first)
        lam_in = sb("lam_in", [P, LAYERS, 4, HD], F32, first)
        lam_p = sb("lam_p", [P, LAYERS, 2, HD], F32, first)
        lam_s = sb("lam_s", [P, LAYERS, 2], F32, first)
        mask = sb("mask", [P, 384], F32, first)
        ang = sb("ang", [P, 2, T], F32, first)
        turns = sb("turns", [P, 2, T], F32, first)
        pos_i = turns[:, 1, :].bitcast(I32)
        ada_pre = sb("ada_pre", [P, ADA_FIRST, 2, 1024], F32, first)
        first.close()

        mix = ExitStack()
        G = sb("G", [P, 24, T], F32, mix)
        latq = sb("latq", [P, QT + KVT, T], F32, mix)
        latH = sb("latH", [P, QT + KVT, T], F32R, mix)
        latL = sb("latL", [P, QT + KVT, T], F32R, mix)
        qraw = sb("qraw", [P, 2, T], F32, mix)
        rot_s = sb("rot_s", [P, 2, T], F32, mix)
        qD = sb("qD", [P, 2, T], F32, mix)
        kM = sb("kM", [P, 2, T], F32, mix)
        vM = [sb(f"vM{i}", [P, 2, P], F32, mix) for i in range(2)]
        W = sb("W", [P, 2, 384], F32, mix)
        PT = sb("PT", [P, 384], F32, mix)
        nmax = sb("nmax", [P, 4], F32, mix)
        nb = sb("nb", [P, 4], F32, mix)
        esum = sb("esum", [P, 4], F32, mix)
        rsum = sb("rsum", [P, 4], F32, mix)
        oBH = sb("oBH", [P, HEADS_D, T], F32R, mix)
        oBL = sb("oBL", [P, HEADS_D, T], F32R, mix)
        oAH = sb("oAH", [P, HEADS_M // 2, T], F32R, mix)
        oAL = sb("oAL", [P, HEADS_M // 2, T], F32R, mix)
        uH = sb("uH", [P, CT, T], F32R, mix)
        uL = sb("uL", [P, CT, T], F32R, mix)
        mix.close()
        lat = buf[:, 0:QT + KVT, :]
        cv = buf[:, 0:CT, :]
        oB = buf[:, CT:CT + HEADS_D, :]
        ln_th = buf[:, CT:2 * CT, :]
        oBq = latq[:, 0:HEADS_D, :]
        flat_xn = xn[:, :, :].rearrange("p k t -> p (k t)")
        vD = [flat_xn[:, i * 512:(i + 1) * 512].rearrange("p (k t) -> p k t", k=2) for i in range(2)]
        E = flat_xn[:, 1024:1024 + 768].rearrange("p (m s) -> p m s", m=2)
        late = G[:, 12:24, :].rearrange("p k t -> p (k t)")
        kraw = late[:, 0:512].rearrange("p (k t) -> p k t", k=2)
        kD = late[:, 512:1024].rearrange("p (k t) -> p k t", k=2)
        cth = late[:, 1024:1536].rearrange("p (k t) -> p k t", k=2)
        krope = late[:, 1536:1536 + T]
        up_pad = late[:, 1792:1792 + CT * (TAPS - 1 + T)].rearrange("p (k t) -> p k t", k=CT)
        qM = qD
        mlp = ExitStack()
        gH = sb("gH", [P, FT, T], F32R, mlp)
        gL = sb("gL", [P, FT, T], F32R, mlp)
        ca = sb("ca", [P, 2, T], F32, mlp)
        cb = sb("cb", [P, 2, T], F32, mlp)
        th = sb("th", [P, 2, T], F32, mlp)
        gy = sb("gy", [P, 2, T], F32, mlp)
        mlp.close()

        PB = [bank("PB0"), bank("PB1")]
        SC = [bank("SC0"), bank("SC1")]
        TR = bank("TR")
        OB = bank("OB")
        ST = bank("ST")
        MI = bank("MI")
        DN = [SC[0], SC[1], TR, OB]
        OUT = [PB, SC]

        s_cst, s_mask, s_x, s_pos, s_lam, s_vec = sem("cst_in"), sem("mask_in"), sem("x_in"), sem("pos_in"), sem("lam_in_s"), sem("vec_in")
        raw_in = [sem(f"raw_in{i}") for i in range(RAW)]
        w_hi = sem("w_hi")
        w_lo = [sem(f"w_lo{i}") for i in range(RAW)]
        w_lo_pool = [sem(f"w_lo_pool{i}") for i in range(RAW)]
        pb_full, pb_read = sem("pb_full"), [sem("pb_read0"), sem("pb_read1")]
        tr_full, tr_read = sem("tr_full"), sem("tr_read")
        ob_full, ob_read = sem("ob_full"), sem("ob_read")
        st_full, st_read = sem("st_full"), sem("st_read")
        mi_full, mi_read = sem("mi_full"), sem("mi_read")
        sc_full, e_ready = sem("sc_full"), sem("e_ready")
        ada_in, ada_used, ada_half = sem("ada_in"), sem("ada_used"), sem("ada_half")
        ada_pre_in = [sem(f"ada_pre_in{i}") for i in range(ADA_FIRST)]
        acc_clear, v_link, p_link = sem("acc_clear"), sem("v_link"), sem("p_link")
        s_const, s_ones, s_xtr, s_vtr, s_vt = sem("const_made"), sem("ones_made"), sem("x_turned"), sem("vec_turned"), sem("vecs_made")
        s_cth, s_ang, s_table, s_lame, s_lamx = sem("c_tanh"), sem("angles"), sem("tables"), sem("lam_sums"), sem("lam_exp")
        x_ready, sq_ready, xn_ready, h_hi, h_lo = sem("x_ready"), sem("sq_ready"), sem("xn_ready"), sem("h_hi"), sem("h_lo")
        lat_y, lat_hi, lat_lo = sem("lat_y"), sem("lat_hi"), sem("lat_lo")
        roped, nb_ready, w_ready = sem("roped"), sem("nb_ready"), sem("w_ready")
        o_hi, sub_y, sub_hi, sub_lo = sem("o_hi"), sem("sub_y"), sem("sub_hi"), sem("sub_lo")
        conv_done, cen_ready, cen_sq, ln_y, ln_t, ln_u, ln_hi, ln_lo = (
            sem(n) for n in ("conv_done", "centred", "centred_sq", "ln_y", "ln_t", "ln_u", "ln_hi", "ln_lo"))
        m_ready, m_hi, m_lo = sem("merged"), sem("merged_hi"), sem("merged_lo")
        tap_ready, th_ready, gy_ready, g_hi, g_lo = (
            sem(n) for n in ("up_tap", "up_tanh", "up_gated", "gated_hi", "gated_lo"))
        down_used, fin_y, out_turned, s_out = (sem(n) for n in ("down_used", "fin_y", "out_turned", "out_done"))
        down_done, s_silu, s_cvec, s_abs, touched = (
            sem(n) for n in ("down_done", "silu_c", "c_in", "abs_made", "touched"))
        out_ready = [sem("out_ready0"), sem("out_ready1")]

        def vector_share(n):
            return chunk_size(n) * (SHARE_UP if n >= UP else SHARE) // 8

        by_rows = lambda v: v.rearrange("l (k p) -> k l p", p=P)
        vectors = [(V_ADAB, 0, by_rows(ada_b)), (V_N1, 0, by_rows(norm1_g)), (V_N2, 0, by_rows(norm2_g)),
                   (V_QG, 0, by_rows(q_norm_g)), (V_KVG, 0, by_rows(kv_norm_g)), (V_CB, 0, by_rows(conv_dw_b)),
                   (V_LNG, 0, by_rows(conv_ln_g)), (V_LNB, 0, by_rows(conv_ln_b)), (V_SUB, 0, by_rows(diff_subln_g)),
                   (V_FB, 0, by_rows(ffn_conv_b)),
                   (0, 1, conv_dw_w.rearrange("l k (c p) -> (k c) l p", p=P)),
                   (0, 2, ffn_conv_w[:, 0:2, :].rearrange("l k (c p) -> (k c) l p", p=P)),
                   (0, 3, ffn_conv_w[:, 2, :].rearrange("l (c p) -> c l p", p=P))]
        assert len(vectors) == VEC_LOADS

        def load_vectors(eng, some):
            for at, q, v in some:
                eng.dma_start(rows[at:at + v.shape[0], q:8:4, :], v).then_inc(s_vec, 16)

        block = stack.enter_context(nc.Block())

        @block.sync
        def _(sp):
            sp.sem_inc(down_used, RAW)
            for s in (*pb_read, ob_read, tr_read, st_read, e_ready, gy_ready, touched):
                sp.sem_inc(s, FREE)
            in_v = w_in.rearrange("l (k p) c -> l p k c", p=P)
            uq_v = w_uq.rearrange("l (k p) c -> l p k c", p=P)
            ukv_v = w_ukv.rearrange("l (k p) c -> l p k c", p=P)
            outs_v = [w.rearrange("l (k p) c -> l p k c", p=P) for w in (w_out_diff, w_out_conv, w_out_mla)]
            wo_v = w_o.rearrange("l (k p) c -> l p k c", p=P)
            up_v = w_up.rearrange("l (k p) c -> l p k c", p=P)
            down_v = w_down.rearrange("l (k p) c -> l p k c", p=P)
            ada_v = ada_w.rearrange("l (k p) c -> p (l k) c", p=P)

            def load(l, n, r=0):
                s = n % RAW
                if n < RAW:
                    sp.wait_ge(down_used, RAW + l * (FT // 2) + n - RAW + 1)
                elif n - RAW >= DOWN:
                    sp.wait_ge(down_used, RAW + l * (FT // 2) + n - RAW - DOWN + 1)
                else:
                    where, count = last_use(n - RAW)
                    if where == "pb":
                        sp.wait_ge(pb_full, l * PB_USES + count + 4 * r)
                    else:
                        sp.wait_ge(ob_full, l * len(OB_USES) + count)
                if n < LAT + 2:
                    src = in_v[l, :, :, n * 256:(n + 1) * 256]
                elif n == LAT + 2:
                    src = in_v[l, :, :, 512:512 + P + ROPE]
                elif n < MLA:
                    i, what = divmod(n - DIFF, 5)
                    col = (COL_DQ, COL_DK, COL_DV, COL_CONV_G, COL_CONV_A)[what] + 256 * i
                    src = in_v[l, :, :, col:col + 256]
                elif n < OUTS:
                    p, what = divmod(n - MLA, 5)
                    g = gate_of(n)
                    if what == 0:
                        src = uq_v[l, :, :, 192 * p:192 * (p + 1)]
                    elif what == 2:
                        src = ukv_v[l, :, :, 256 * p:256 * (p + 1)]
                    else:
                        src = in_v[l, :, :, COL_GATE + 256 * g:COL_GATE + 256 * (g + 1)]
                elif n < WO:
                    b, half = divmod(n - OUTS, 2)
                    src = outs_v[b][l, :, :, 512 * half:512 * (half + 1)]
                elif n < UP:
                    src = wo_v[l, :, :, 256 * (n - WO):256 * (n - WO + 1)]
                elif n < DOWN:
                    i, b = divmod(n - UP, 2)
                    src = up_v[l, :, :, bass.ds(r * 512 + (i * 256 + b * FF), 256)]
                else:
                    src = down_v[l, :, 2 * (n - DOWN):2 * (n - DOWN) + 2, :]
                k, w = src.shape[-2], src.shape[-1]
                sp.dma_start(raw[s][:, 0:k * w].rearrange("p (k c) -> p k c", k=k), src).then_inc(raw_in[s], 16)

            def load_ada(l, a, r=0):
                part, i = ADA_PARTS[a // ADA_PART], a % ADA_PART
                if a == 0:
                    sp.wait_ge(mi_full, 2 + l * 6)
                sp.wait_ge(ada_used, ADA_FIRST + l * ADA_CHUNKS + a + r)
                if a < ADA_NEXT:
                    src = ada_v[:, bass.ds(l * DT + 2 * r + 2 * i, 2), 1024 * part:1024 * (part + 1)]
                else:
                    src = ada_v[:, (LAYERS - 1) * DT + 2 * i:(LAYERS - 1) * DT + 2 * i + 2,
                                1024 * part:1024 * (part + 1)]
                sp.dma_start(ada[:, :, :], src).then_inc(ada_in, 16)

            sp.dma_start(xn[:, :, :].rearrange("p (a k) t -> p a (k t)", a=2),
                         x[0, :, :].rearrange("(a p) d -> p a d", p=P)).then_inc(s_x, 16)
            sp.dma_start(pos_i[:, :], positions.broadcast_to([P, T])).then_inc(s_pos, 16)
            sp.dma_start(mask[:, :], consts[:, C_MASK:NC_CONST]).then_inc(s_mask, 16)
            sp.dma_start(lam_in[:, :, :, :].rearrange("p l a b -> p (l a b)"),
                         diff_lambda.rearrange("(o l) a b -> o (l a b)", o=1).broadcast_to([P, LAYERS * 4 * HD])).then_inc(s_lam, 16)
            for a in range(ADA_FIRST):
                load_vectors(sp, vectors[1 + 4 * a:5 + 4 * a] if a in (1, 2) else [])
                part, i = divmod(a, ADA_PART)
                sp.dma_start(ada_pre[:, a, :, :],
                             ada_v[:, 2 * i:2 * i + 2, 1024 * part:1024 * (part + 1)]).then_inc(ada_pre_in[a], 16)

            def ada_behind(l, n):
                if n not in ADA_LOADS:
                    return
                a = ADA_LOADS.index(n)
                if a < ADA_NEXT:
                    load_ada(l, a)
                else:
                    with sp.If(l < LAYERS - 1):
                        load_ada(l, a)

            with sp.Fori(0, LAYERS) as l:
                for n in range(UP):
                    load(l, n)
                    ada_behind(l, n)
                with sp.Fori(0, UP_LOOPS) as r:
                    for j in range(4):
                        load(l, UP + j, r)
                    load_ada(l, ADA_LOOP, r)
                for n in range(UP + 4 * UP_LOOPS, CHUNKS):
                    load(l, n)
                    ada_behind(l, n)

            for a in range(2):
                sp.wait_ge(out_ready[a], 2)
                sp.dma_start(out[0, a * P:(a + 1) * P, :],
                             xn[:, 4 * a:4 * a + 4, :].rearrange("p k t -> p (k t)")).then_inc(s_out, 16)
            sp.wait_ge(s_out, 32)

        def factors(i):
            return c_act[:, 2, 2 * i:2 * i + 2]

        @block.gpsimd
        def _(pool):
            chain = Chain(pool, p_link)
            link = chain.link
            pool.wait_ge(s_cst, 16)
            pool.wait_ge(s_mask, 16)
            pool.tensor_copy(maskb[:, :], mask[:, :])
            pool.tensor_copy(identb[:, :], ident).then_inc(s_const, 1)
            pool.wait_ge(s_pos, 16)
            link(pool.tensor_copy(turns[:, 0, :], pos_i[:, :]))
            pool.tensor_scalar(ang[:, 1, :], turns[:, 0, :], cst[:, C_INV + 1:C_INV + 2], None, ALU.mult)
            link(pool.tensor_scalar(ang[:, 0, :], turns[:, 0, :], cst[:, C_INV:C_INV + 1], None, ALU.mult))
            link(pool.tensor_scalar(turns[:, :, :], ang[:, :, :], 1.0 / (2 * math.pi), ROUND, ALU.mult, ALU.add))
            link(pool.tensor_scalar(turns[:, :, :], turns[:, :, :], ROUND, None, ALU.subtract))
            flat2 = lambda t: t[:, :, :].rearrange("p k t -> p (k t)")
            for part in (TWO_PI_1, TWO_PI_2, TWO_PI_3):
                link(pool.tensor_scalar(rdev[:, :], flat2(turns), -part, None, ALU.mult))
                link(pool.tensor_tensor(flat2(ang), flat2(ang), rdev[:, :], ALU.add))
            edge = float(np.nextafter(np.float32(math.pi), np.float32(0)))
            pool.tensor_scalar(ang[:, :, :], ang[:, :, :], edge, -edge, ALU.min, ALU.max).then_inc(s_ang, 1)

            def low(l, n, r=0):
                s, cut, size = n % RAW, vector_share(n), chunk_size(n)
                pool.wait_ge(w_hi, l * CHUNKS + n + 1 + 4 * r)
                pool.tensor_tensor(wL[s][:, cut:size], raw[s][:, cut:size], wH[s][:, cut:size].bitcast(F32),
                                   ALU.subtract).then_inc(w_lo_pool[s], 1)

            with pool.Fori(0, LAYERS) as l:
                for n in range(UP + 2):
                    low(l, n)
                with pool.Fori(0, UP_LOOPS) as r:
                    for j in range(4):
                        low(l, UP + 2 + j, r)
                for n in range(UP + 4 * UP_LOOPS + 2, CHUNKS):
                    low(l, n)

        @block.scalar
        def _(act):
            act.dma_start(rows[0:DT, 8, :], c[0, :].rearrange("(k p) -> k p", p=P)).then_inc(s_cvec, 16)
            act.dma_start(cst[:, :], consts[:, 0:C_MASK]).then_inc(s_cst, 16)
            act.dma_start(rows[DT:2 * DT, 8, :], final_g.rearrange("(k p) -> k p", p=P)).then_inc(s_cvec, 16)
            load_vectors(act, vectors[0:5])

            act.wait_ge(s_vt, 1)
            act.activation(c_act[:, 1, :], c_act[:, 0, :], ACT.Tanh, scale=0.5).then_inc(s_cth, 1)
            for l in range(LAYERS):
                act.wait_ge(s_vtr, 2 + l)
                for at, count, b in ((0, ROWS_A, 0), (V_CW, ROWS_B, P), (V_FW, 4 * FT, 2 * P), (V_FW + 4 * FT, 2 * FT, 3 * P)):
                    ins = act.activation(vec_all[:, l, at:at + count], PB[l][:, b:b + count], ACT.Copy)
                ins.then_inc(s_vt, 1)
            act.wait_ge(s_lame, 1)
            act.activation(lam_s[:, :, :], lam_s[:, :, :], ACT.Exp).then_inc(s_lamx, 1)
            def squares(l, which):
                for k in range(DT):
                    if which == 0:
                        act.wait_ge(x_ready, l * DT + k + 1)
                    elif k % 2 == 0:
                        u = PB_WO + k // 2
                        act.wait_ge(pb_read[u % 2], FREE + l * (PB_USES // 2) + u // 2 + 1)
                    act.activation(buf[:, k, :], xT[:, k, :], ACT.Square).then_inc(sq_ready, 1)

            squares(0, 0)
            act.wait_ge(s_ang, 1)
            act.wait_ge(s_ones, 1)
            act.activation(turns[:, :, :], ang[:, :, :], ACT.Abs).then_inc(s_abs, 1)
            act.activation(sin[:, :, :], ang[:, :, :], ACT.Sin)
            act.wait_ge(s_abs, 1)
            act.activation(cos[:, :, :], turns[:, :, :], ACT.Sin, bias=half_pi[:, :], scale=-1.0).then_inc(s_table, 1)

            def high(l, n, r=0):
                s, size = n % RAW, chunk_size(n)
                act.wait_ge(raw_in[s], (l * (CHUNKS // RAW) + n // RAW + 1 + r) * 16)
                act.activation(wH[s][:, 0:size], raw[s][:, 0:size], ACT.Copy).then_inc(w_hi, 1)

            def full(l, u, r=0):
                act.wait_ge(pb_full, l * PB_USES + u + 1 + 4 * r)
                return PB[u % 2]

            def st_done(l, use):
                act.wait_ge(st_full, l * len(ST_USES) + ST_USES.index(use) + 1)

            def root(l, which):
                act.wait_ge(st_full, l * len(ST_USES) + ST_USES.index(("N1", "N2")[which]) + 1)
                act.activation(rdev[:, 0:T], ST[:, 0:T], ACT.Sqrt, bias=eps[:, :], scale=1.0 / D).then_inc(st_read, 1)
                act.wait_ge(touched, FREE + 2 * l + which)
                act.activation(touch[:, :], eps[:, :], ACT.Tanh).then_inc(touched, 1)

            def shifted(l, which):
                for k in range(DT):
                    act.wait_ge(xn_ready, l * 2 * DT + which * DT + k + 1)
                    shift = mod[:, 3 * which * DT + k:3 * which * DT + k + 1]
                    act.activation(hH[:, k, :], xn[:, k, :], ACT.Identity, bias=shift).then_inc(h_hi, 1)

            def exps(l, use):
                act.wait_ge(nb_ready, l * len(SC_USES) + SC_USES.index(use) + 1)
                scale = SCALE_D if use[0] == "D" else SCALE_M
                for m in range(2):
                    for b, (lo, hi) in enumerate(((0, 128), (128, 384))):
                        i = 2 * m + b
                        ins = act.activation(E[:, m, lo:hi], SC[m][:, lo:hi], ACT.Exp, bias=nb[:, i:i + 1], scale=scale,
                                             accum_out=esum[:, i:i + 1])
                ins.then_inc(e_ready, 1)

            def mixer_step(l, n):
                high(l, n + 2)
                if n - 1 in SCORES_AT:
                    exps(l, SCORES_AT[n - 1])
                if n < LAT + 3:
                    m = 1 if n == 2 else 2
                    b = full(l, n)
                    src = b[:, 0:m * T].rearrange("p (k t) -> p k t", k=m)
                    act.activation(lat[:, 2 * n:2 * n + m, :], src, ACT.Copy)
                    act.activation(latq[:, 2 * n:2 * n + m, :], src, ACT.Square).then_inc(pb_read[n % 2], 1)
                    if n == 2:
                        b = full(l, 3)
                        act.activation(krope[0:96, :], b[0:96, 0:T], ACT.Copy).then_inc(pb_read[1], 1)
                elif n < MLA:
                    i, what = divmod(n - DIFF, 5)
                    if what in (0, 1):
                        b = full(l, PB_DIFF + 4 * i + what)
                        act.activation((qraw, kraw)[what][:, :, :].rearrange("p k t -> p (k t)"), b[:, :],
                                       ACT.Copy).then_inc(pb_read[what], 1)
                    elif what == 2:
                        act.wait_ge(ob_full, l * len(OB_USES) + OB_USES.index(f"V{i}") + 1)
                        act.activation(vD[i][:, :, :].rearrange("p k t -> p (k t)"), OB[:, :], ACT.Copy).then_inc(ob_read, 1)
                    elif what == 3:
                        b = full(l, PB_DIFF + 4 * i + 2)
                        act.activation(cth[:, :, :].rearrange("p k t -> p (k t)"), b[:, :], ACT.Tanh,
                                       scale=0.5).then_inc(pb_read[0], 1)
                elif n < OUTS:
                    p, what = divmod(n - MLA, 5)
                    u = PB_MLA + 5 * p + what
                    if what == 0:
                        b = full(l, u)
                        act.activation(qraw[0:96, :, :].rearrange("p k t -> p (k t)"), b[0:96, :],
                                       ACT.Copy).then_inc(pb_read[u % 2], 1)
                    elif what == 2:
                        b = full(l, u)
                        act.activation(kM[0:NOPE, :, :].rearrange("p k t -> p (k t)"), b[0:NOPE, :],
                                       ACT.Copy).then_inc(pb_read[u % 2], 1)
                        act.wait_ge(ob_full, l * len(OB_USES) + OB_USES.index(f"VM{p}") + 1)
                        act.activation(vM[p % 2][:, :, :].rearrange("p k t -> p (k t)"), OB[:, 0:256],
                                       ACT.Copy).then_inc(ob_read, 1)
                    else:
                        b, g = full(l, u), gate_of(n)
                        act.activation(G[:, 2 * g:2 * g + 2, :].rearrange("p k t -> p (k t)"), b[:, :], ACT.Tanh,
                                       scale=0.5).then_inc(pb_read[u % 2], 1)
                if n in VALUES_AT:
                    use = VALUES_AT[n]
                    act.wait_ge(ob_full, l * len(OB_USES) + OB_USES.index(use) + 1)
                    if use[1] == "D":
                        h = int(use[2])
                        act.activation(oB[:, h, :], OB[:, 0:T], ACT.Copy)
                        act.activation(oBq[:, h, :], OB[:, 0:T], ACT.Square).then_inc(ob_read, 1)
                    else:
                        p, r0 = int(use[2]), 0 if use[3] == "A" else 64
                        act.activation(oAH[r0:r0 + 64, p, :], OB[r0:r0 + 64, 0:T], ACT.Copy).then_inc(o_hi, 1)
                if n in TRANSPOSE_AT:
                    act.wait_ge(tr_full, l * len(TR_USES) + TR_USES.index(TRANSPOSE_AT[n]) + 1)
                    act.activation(PT[:, :], TR[:, 0:384], ACT.Copy).then_inc(tr_read, 1)
                use = STATS_AT.get(n)
                if use == "LAT":
                    st_done(l, use)
                    act.activation(rdev[:, 0:T], ST[:, 0:T], ACT.Sqrt, bias=eps[:, :], scale=1.0 / QR)
                    act.activation(rdev[:, T:2 * T], ST[:, T:2 * T], ACT.Sqrt, bias=eps[:, :],
                                   scale=1.0 / KVR).then_inc(st_read, 1)
                elif use in ("SUB0", "SUB1"):
                    st_done(l, use)
                    act.activation(rdev[:, :], ST[:, :], ACT.Sqrt, bias=eps[:, :], scale=1.0 / P).then_inc(st_read, 1)
                elif use == "LNQ":
                    st_done(l, use)
                    act.activation(rdev[:, 0:T], ST[:, 0:T], ACT.Sqrt, bias=eps[:, :], scale=1.0 / CONV_CH).then_inc(st_read, 1)
                if n == 5:
                    act.wait_ge(lat_y, l + 1)
                    act.activation(latH[:, :, :].rearrange("p k t -> p (k t)"), lat[:, :, :].rearrange("p k t -> p (k t)"),
                                   ACT.Copy).then_inc(lat_hi, 1)
                if n in (19, 24):
                    i = (19, 24).index(n)
                    act.wait_ge(sub_y, l * 2 + i + 1)
                    act.activation(oBH[:, 2 * i:2 * i + 2, :].rearrange("p k t -> p (k t)"),
                                   oBq[:, 2 * i:2 * i + 2, :].rearrange("p k t -> p (k t)"), ACT.Copy).then_inc(sub_hi, 1)
                if n == 27:
                    act.wait_ge(cen_ready, l + 1)
                    act.activation(latq[:, 0:CT, :].rearrange("p k t -> p (k t)"), cv[:, :, :].rearrange("p k t -> p (k t)"),
                                   ACT.Square).then_inc(cen_sq, 1)
                if n == 30:
                    act.wait_ge(ln_y, l + 1)
                    for t in range(CT):
                        act.activation(cv[:, t, :], latq[:, t, :], ACT.Identity, bias=vec[:, V_LNB + t:V_LNB + t + 1])
                        ins = act.activation(ln_th[:, t, :], latq[:, t, :], ACT.Tanh, bias=half_b[:, t:t + 1],
                                             scale=0.5)
                    ins.then_inc(ln_t, 1)
                if n == 32:
                    act.wait_ge(ln_u, l + 1)
                    act.activation(uH[:, :, :].rearrange("p k t -> p (k t)"), latq[:, 0:CT, :].rearrange("p k t -> p (k t)"),
                                   ACT.Copy, scale=0.5).then_inc(ln_hi, 1)

            def up_step(l, n, r=0):
                i, b = divmod(n - UP, 2)
                if b == 1:
                    high(l, n + 2, r)
                    act.wait_ge(pb_read[0], FREE + l * (PB_USES // 2) + (PB_UP + n - UP) // 2 + 1 + 2 * r)
                    act.activation(th[:, :, :].rearrange("p k t -> p (k t)"), ca[:, :, :].rearrange("p k t -> p (k t)"),
                                   ACT.Tanh, scale=0.5).then_inc(th_ready, 1)
                pb = full(l, PB_UP + n - UP, r)
                dst = (ca, cb)[b]
                act.wait_ge(gy_ready, FREE + l * (FT // 2) + i + 2 * r)
                for t in range(2):
                    col = b * FT + 2 * i + t
                    ins = act.activation(dst[:, t, :], pb[:, t * T:(t + 1) * T], ACT.Identity,
                                         bias=vec[:, bass.ds(V_FB + col + 4 * r, 1)],
                                         scale=vec[:, bass.ds(V_FW + 2 * 2 * FT + col + 4 * r, 1)])
                ins.then_inc(tap_ready, 1)
                if b == 0:
                    high(l, n + 2, r)
                if b == 1:
                    act.wait_ge(gy_ready, FREE + l * (FT // 2) + i + 1 + 2 * r)
                    act.activation(gH[:, bass.ds(2 * i + 4 * r, 2), :].rearrange("p k t -> p (k t)"),
                                   gy[:, :, :].rearrange("p k t -> p (k t)"), ACT.Copy).then_inc(g_hi, 1)

            root(0, 0)
            high(0, 0)
            high(0, 1)
            with act.Fori(0, LAYERS) as l:
                shifted(l, 0)
                for n in range(WO):
                    mixer_step(l, n)
                    if n >= WO - 2:
                        for u in range(2):
                            i = 2 * (n - (WO - 2)) + u
                            act.wait_ge(m_ready, l * 4 + i + 1)
                            act.activation(hH[:, 2 * i:2 * i + 2, :].rearrange("p k t -> p (k t)"),
                                           buf[:, 2 * i:2 * i + 2, :].rearrange("p k t -> p (k t)"), ACT.Copy,
                                           scale=0.5).then_inc(m_hi, 1)
                for n in range(WO, UP):
                    high(l, n + 2)
                squares(l, 1)
                root(l, 1)
                shifted(l, 1)
                with act.Fori(0, UP_LOOPS) as r:
                    for j in range(4):
                        up_step(l, UP + j, r)
                for n in range(UP + 4 * UP_LOOPS, DOWN):
                    up_step(l, n)
                for n in range(DOWN, CHUNKS - 2):
                    high(l, n + 2)
                with act.If(l < LAYERS - 1):
                    high(l + 1, 0)
                    high(l + 1, 1)
                squares(l + 1, 0)
                root(l + 1, 0)

            for a in range(2):
                act.wait_ge(out_turned, 2 * a + 2)
                act.activation(xn[:, 4 * a + 2:4 * a + 4, :].rearrange("p k t -> p (k t)"), OUT[a][1][:, :],
                               ACT.Copy).then_inc(out_ready[a], 1)

        @block.vector
        def _(dve):
            chain = Chain(dve, v_link)
            link = chain.link

            dve.memset(ones[:, :], 1.0)
            dve.memset(half_pi[:, :], math.pi / 2)
            dve.memset(eps[:, :], EPS).then_inc(s_ones, 1)
            dve.wait_ge(s_vtr, 1)
            dve.tensor_copy(c_act[:, 0, :], MI[:, 0:DT])
            dve.tensor_copy(fin_g[:, :], MI[:, DT:2 * DT]).then_inc(s_vt, 1)
            dve.wait_ge(s_cth, 1)
            dve.wait_ge(s_vt, 1)
            link(dve.scalar_tensor_tensor(c_act[:, 2, :], c_act[:, 1, :], 1.0, c_act[:, 0, :], ALU.add, ALU.mult))
            dve.tensor_scalar_mul(c_act[:, 2, :], c_act[:, 2, :], 0.5).then_inc(s_silu, 1)
            for b in range(4):
                dve.wait_ge(s_xtr, b + 1)
                dve.tensor_copy(xT[:, 2 * b:2 * b + 2, :].rearrange("p k t -> p (k t)"), DN[b][:, :]).then_inc(x_ready, 2)
            def ada_end(part, order, source):
                dve.wait_ge(mi_full, order)
                dve.tensor_tensor(mod[:, part * DT:(part + 1) * DT], MI[:, 0:DT],
                                  source[:, V_ADAB + part * DT:V_ADAB + (part + 1) * DT], ALU.add).then_inc(mi_read, 1)

            def ada_products(src, factor, halves, first, acc=acc):
                if first:
                    ins = dve.tensor_scalar(acc[:, :], src[:, 0, :], factor[:, 0:1], None, ALU.mult)
                else:
                    ins = dve.scalar_tensor_tensor(acc[:, :], src[:, 0, :], factor[:, 0:1], acc[:, :], ALU.mult, ALU.add)
                ins.then_inc(ada_half, 1)
                dve.wait_ge(ada_half, halves)
                dve.scalar_tensor_tensor(acc[:, :], src[:, 1, :], factor[:, 1:2], acc[:, :], ALU.mult,
                                         ALU.add).then_inc(ada_used, 1)

            def ada_step(l, a, r=0):
                serial = ADA_FIRST + l * ADA_CHUNKS + a + r
                dve.wait_ge(ada_in, (l * ADA_CHUNKS + a + 1) * 16 + 16 * r)
                if a == ADA_LOOP:
                    dve.wait_ge(acc_clear, l + 1)
                elif a % ADA_PART == 0:
                    dve.wait_ge(mi_full, 2 + l * 6 + a // ADA_PART)
                dve.wait_ge(ada_used, serial)
                factor = c_act[:, 2, bass.ds(2 * r, 2)] if a == ADA_LOOP else factors(a % ADA_PART)
                ada_products(ada, factor, serial + 1, a % ADA_PART == 0 and a != ADA_LOOP)

            dve.wait_ge(s_silu, 1)
            for a in range(ADA_FIRST):
                dve.wait_ge(ada_pre_in[a], 16)
                if a:
                    dve.wait_ge(ada_used, a)
                ada_products(ada_pre[:, a, :, :], factors(a % ADA_PART), a + 1, a % ADA_PART == 0,
                             acc if a < ADA_PART else acc_pre)
                if a == 2:
                    dve.wait_ge(s_lam, 16)
                    for l in range(LAYERS):
                        ins = dve.tensor_tensor(lam_p[:, l, :, :], lam_in[:, l, 0::2, :], lam_in[:, l, 1::2, :], ALU.mult)
                    link(ins)
                    dve.tensor_reduce(lam_s[:, :, :], lam_p[:, :, :, :], AX.X, ALU.add).then_inc(s_lame, 1)
                    for l in range(LAYERS):
                        ins = dve.tensor_copy(vec_all[:, l, V_LAM:V_LAM + 2], cst[:, C_LAM + 2 * l:C_LAM + 2 * l + 2])
                    link(ins)
                if a == 6:
                    dve.wait_ge(s_lamx, 1)
                    link(dve.tensor_tensor(lamb[:, 0, :], lam_s[:, :, 1], lam_s[:, :, 0], ALU.subtract))
                    link(dve.tensor_tensor(lamb[:, 1, :], lamb[:, 0, :], vec_all[:, :, V_LAM], ALU.subtract))
            dve.wait_ge(s_vt, 1 + LAYERS)
            ada_end(0, 1, vec_all[:, 0, :])

            def low(l, n, r=0):
                s, cut = n % RAW, vector_share(n)
                dve.wait_ge(w_hi, l * CHUNKS + n + 1 + 4 * r)
                dve.tensor_tensor(wL[s][:, 0:cut], raw[s][:, 0:cut], wH[s][:, 0:cut].bitcast(F32),
                                  ALU.subtract).then_inc(w_lo[s], 1)

            def flat(t):
                return t.rearrange("p k t -> p (k t)")

            def norm(l, which):
                dve.wait_ge(st_read, FREE + l * len(ST_USES) + (1, 7)[which])
                link(dve.reciprocal(rdev[:, 0:T], rdev[:, 0:T]))
                for k in range(DT + 2):
                    if k < DT:
                        dve.scalar_tensor_tensor(xn[:, k, :], xT[:, k, :], gs[:, which, k:k + 1], rdev[:, 0:T], ALU.mult,
                                                 ALU.mult).then_inc(xn_ready, 1)
                    if k >= 2:
                        j = k - 2
                        dve.wait_ge(h_hi, l * 2 * DT + which * DT + j + 1)
                        dve.scalar_tensor_tensor(hL[:, j, :], xn[:, j, :], mod[:, 3 * which * DT + j:3 * which * DT + j + 1],
                                                 hH[:, j, :].bitcast(F32), ALU.add, ALU.subtract).then_inc(h_lo, 1)

            def rope(l, use):
                i = int(use[2]) if use[1] != "k" or use[2] != "r" else 0
                if use == "Rkr":
                    src, n0, n1, which, u = krope, 64, 96, 1, 3
                elif use[1] == "M":
                    src, n0, n1, which, u = qraw, 0, 96, 1, PB_MLA + 5 * i
                else:
                    src, n0, n1, which, u = (qraw, kraw)[use[1] == "k"], 0, P, 0, PB_DIFF + 4 * i + (use[1] == "k")
                dve.wait_ge(pb_read[u % 2], FREE + l * (PB_USES // 2) + u // 2 + 1)
                turned = l * len(TR_USES) + TR_USES.index(use) + 1
                if use == "Rkr":
                    dve.tensor_tensor(kM[64:96, 0, :], krope[64:96, :], cos[64:96, 1, :], ALU.mult)
                    dve.wait_ge(tr_full, turned)
                    dve.tensor_tensor(rot_s[64:96, 0, :], TR[64:96, 0:T], sin[64:96, 1, :], ALU.mult).then_inc(tr_read, 1)
                    dve.wait_ge(tr_read, FREE + turned)
                    link(dve.tensor_tensor(kM[64:96, 0, :], kM[64:96, 0, :], rot_s[64:96, 0, :], ALU.add))
                    link(dve.tensor_copy(kM[64:96, 1, :], kM[64:96, 0, :]))
                    return
                dst = {"q": qD, "k": kD, "M": qM}[use[1]][n0:n1, :, :]
                c, s = (t[n0:n1, which, :].unsqueeze(1).broadcast_to([n1 - n0, 2, T]) for t in (cos, sin))
                dve.wait_ge(tr_full, turned)
                dve.tensor_tensor(dst, src[n0:n1, :, :], c, ALU.mult)
                dve.tensor_tensor(rot_s[n0:n1, :, :], TR[n0:n1, :].rearrange("p (k t) -> p k t", k=2), s,
                                  ALU.mult).then_inc(tr_read, 1)
                dve.wait_ge(tr_read, FREE + turned)
                dve.tensor_tensor(dst, dst, rot_s[n0:n1, :, :], ALU.add).then_inc(roped, 1)
                dve.wait_ge(roped, l * 8 + ROPED.index(use) + 1)

            def row_max(l, use):
                dve.wait_ge(sc_full, l * len(SC_USES) + SC_USES.index(use) + 1)
                for m in range(2):
                    for b, (lo, hi) in enumerate(((0, 128), (128, 384))):
                        i = 2 * m + b
                        ins = dve.tensor_reduce(nmax[:, i:i + 1], SC[m][:, lo:hi], AX.X, ALU.max, negate=True)
                link(ins)
                dve.tensor_scalar_mul(nb[:, :], nmax[:, :], SCALE_D if use[0] == "D" else SCALE_M).then_inc(nb_ready, 1)

            def weights(l, use):
                dve.wait_ge(e_ready, FREE + l * len(SC_USES) + SC_USES.index(use) + 1)
                before = {"D0": None, "M0": "TD3"}.get(use, f"TD{int(use[1]) - 1}" if use[0] == "D" else f"TM{int(use[1]) - 1}B")
                if before:
                    dve.wait_ge(tr_full, l * len(TR_USES) + TR_USES.index(before) + 1)
                link(dve.reciprocal(rsum[:, :], esum[:, :]))
                if use[0] == "D":
                    link(dve.tensor_scalar(rsum[:, 2:4], rsum[:, 2:4], lam_now[:, :], None, ALU.mult))
                    link(dve.tensor_scalar(W[:, 0, 0:128], E[:, 0, 0:128], rsum[:, 0:1], None, ALU.mult), behind=1)
                    link(dve.tensor_scalar(W[:, 0, 128:384], E[:, 0, 128:384], rsum[:, 1:2], None, ALU.mult), behind=1)
                    link(dve.scalar_tensor_tensor(W[:, 0, 0:128], E[:, 1, 0:128], rsum[:, 2:3], W[:, 0, 0:128], ALU.mult,
                                                  ALU.add), behind=1)
                    ins = dve.scalar_tensor_tensor(W[:, 0, 128:384], E[:, 1, 128:384], rsum[:, 3:4], W[:, 0, 128:384],
                                                   ALU.mult, ALU.add)
                else:
                    for m in range(2):
                        dve.tensor_scalar(W[:, m, 0:128], E[:, m, 0:128], rsum[:, 2 * m:2 * m + 1], None, ALU.mult)
                        ins = dve.tensor_scalar(W[:, m, 128:384], E[:, m, 128:384], rsum[:, 2 * m + 1:2 * m + 2], None, ALU.mult)
                ins.then_inc(w_ready, 1)

            def taps(pair, k0, k1):
                for k in range(TAPS - 1 - k0, TAPS - 1 - k1, -1):
                    for t in (2 * pair, 2 * pair + 1):
                        ins = dve.scalar_tensor_tensor(cv[:, t, :], up_pad[:, t, k:k + T],
                                                       vec[:, V_CW + k * CT + t:V_CW + k * CT + t + 1], cv[:, t, :],
                                                       ALU.mult, ALU.add)
                        if (pair, k, t) == (1, 0, CT - 1):
                            ins.then_inc(conv_done, 1)
                        else:
                            link(ins, behind=1)

            def mixer_step(l, n):
                if n < OUTS:
                    low(l, n + 2)
                if n - 1 in SCORES_AT:
                    weights(l, SCORES_AT[n - 1])
                if n in (DIFF + 4, DIFF + 9):
                    i = (n - DIFF) // 5
                    u = PB_DIFF + 4 * i + 3
                    dve.wait_ge(pb_read[0], FREE + l * (PB_USES // 2) + (u - 1) // 2 + 1)
                    dve.wait_ge(pb_full, l * PB_USES + u + 1)
                    dve.scalar_tensor_tensor(up_pad[:, 2 * i:2 * i + 2, TAPS - 1:], cth[:, :, :], 1.0,
                                             PB[1][:, :].rearrange("p (k t) -> p k t", k=2), ALU.add,
                                             ALU.mult).then_inc(pb_read[1], 1)
                    dve.wait_ge(pb_read[1], FREE + l * (PB_USES // 2) + u // 2 + 1)
                    for t in (2 * i, 2 * i + 1):
                        ins = dve.tensor_scalar(cv[:, t, :], up_pad[:, t, TAPS - 1:],
                                                vec[:, V_CW + (TAPS - 1) * CT + t:V_CW + (TAPS - 1) * CT + t + 1],
                                                vec[:, V_CB + t:V_CB + t + 1], ALU.mult, ALU.add)
                    link(ins)
                if n in VALUES_AT and VALUES_AT[n][1] == "M":
                    use = VALUES_AT[n]
                    p, r0 = int(use[2]), 0 if use[3] == "A" else 64
                    dve.wait_ge(o_hi, l * 8 + 2 * p + (use[3] == "B") + 1)
                    dve.tensor_tensor(oAL[r0:r0 + 64, p, :], OB[r0:r0 + 64, 0:T], oAH[r0:r0 + 64, p, :].bitcast(F32),
                                      ALU.subtract).then_inc(ob_read, 1)
                for use in ROTATE_AT.get(n, ()):
                    rope(l, use)
                if n in SCORES_AT:
                    row_max(l, SCORES_AT[n])
                if n == 4:
                    dve.wait_ge(st_read, FREE + l * len(ST_USES) + 2)
                    link(dve.reciprocal(rdev[:, :], rdev[:, :]))
                    for k in range(QT + KVT):
                        g, part = (V_QG + k, 0) if k < QT else (V_KVG + k - QT, T)
                        ins = dve.scalar_tensor_tensor(lat[:, k, :], lat[:, k, :], vec[:, g:g + 1], rdev[:, part:part + T],
                                                       ALU.mult, ALU.mult)
                    ins.then_inc(lat_y, 1)
                if n == 5:
                    dve.memset(up_pad[:, :, 0:TAPS - 1], 0.0)
                if n == 6:
                    dve.wait_ge(lat_hi, l + 1)
                    dve.tensor_tensor(flat(latL[:, :, :]), flat(lat[:, :, :]), flat(latH[:, :, :]).bitcast(F32),
                                      ALU.subtract).then_inc(lat_lo, 1)
                if n in (18, 23):
                    i = (18, 23).index(n)
                    dve.wait_ge(st_read, FREE + l * len(ST_USES) + 3 + i)
                    link(dve.reciprocal(rdev[:, :], rdev[:, :]))
                    dve.scalar_tensor_tensor(flat(oBq[:, 2 * i:2 * i + 2, :]), flat(oB[:, 2 * i:2 * i + 2, :]), sub_g[:, :],
                                             rdev[:, :], ALU.mult, ALU.mult).then_inc(sub_y, 1)
                if n in (20, 25):
                    i = (20, 25).index(n)
                    dve.wait_ge(sub_hi, l * 2 + i + 1)
                    dve.tensor_tensor(flat(oBL[:, 2 * i:2 * i + 2, :]), flat(oBq[:, 2 * i:2 * i + 2, :]),
                                      flat(oBH[:, 2 * i:2 * i + 2, :]).bitcast(F32), ALU.subtract).then_inc(sub_lo, 1)
                if n in TAPS_AT:
                    taps(*TAPS_AT[n])
                if n == 26:
                    dve.wait_ge(st_full, l * len(ST_USES) + 5)
                    dve.tensor_scalar(rdev[:, 0:T], ST[:, 0:T], -1.0 / CONV_CH, None, ALU.mult).then_inc(st_read, 1)
                    dve.wait_ge(st_read, FREE + l * len(ST_USES) + 5)
                    dve.wait_ge(conv_done, l + 1)
                    for k in range(0, CT, 2):
                        ins = dve.tensor_tensor(cv[:, k:k + 2, :], cv[:, k:k + 2, :],
                                                rdev[:, 0:T].unsqueeze(1).broadcast_to([P, 2, T]), ALU.add)
                    ins.then_inc(cen_ready, 1)
                if n == 29:
                    dve.wait_ge(st_read, FREE + l * len(ST_USES) + 6)
                    link(dve.reciprocal(rdev[:, 0:T], rdev[:, 0:T]))
                    for t in range(CT):
                        ins = dve.scalar_tensor_tensor(latq[:, t, :], cv[:, t, :], vec[:, V_LNG + t:V_LNG + t + 1],
                                                       rdev[:, 0:T], ALU.mult, ALU.mult)
                    ins.then_inc(ln_y, 1)
                if n == 31:
                    dve.wait_ge(ln_t, l + 1)
                    dve.scalar_tensor_tensor(flat(latq[:, 0:CT, :]), flat(ln_th), 1.0, flat(cv[:, :, :]), ALU.add,
                                             ALU.mult).then_inc(ln_u, 1)
                if n == 33:
                    dve.wait_ge(ln_hi, l + 1)
                    dve.scalar_tensor_tensor(flat(uL[:, :, :]), flat(latq[:, 0:CT, :]), 0.5, flat(uH[:, :, :]).bitcast(F32),
                                             ALU.mult, ALU.subtract).then_inc(ln_lo, 1)
                if n >= OUTS:
                    b, half = divmod(n - OUTS, 2)
                    for u in range(2):
                        i = 2 * half + u
                        use = PB_OUTS + 2 * (n - OUTS) + u
                        dve.wait_ge(pb_full, l * PB_USES + use + 1)
                        at = (1, 2, 0)[b] * DT + 2 * i
                        g = flat(G[:, at:at + 2, :])
                        dst = flat(buf[:, 2 * i:2 * i + 2, :])
                        to = dst if b == 0 else flat(xn[:, 2 * i:2 * i + 2, :])
                        dve.scalar_tensor_tensor(to, g, 1.0, PB[use % 2][:, :], ALU.add, ALU.mult).then_inc(pb_read[use % 2], 1)
                        if b:
                            dve.wait_ge(pb_read[use % 2], FREE + l * (PB_USES // 2) + use // 2 + 1)
                            ins = dve.tensor_tensor(dst, dst, to, ALU.add)
                            if b == 2:
                                ins.then_inc(m_ready, 1)
                            else:
                                link(ins)
                    low(l, n + 2)
                if n >= WO - 2:
                    for i in range(2 * (n - WO + 2), 2 * (n - WO + 2) + 2):
                        dve.wait_ge(m_hi, l * 4 + i + 1)
                        dve.scalar_tensor_tensor(flat(hL[:, 2 * i:2 * i + 2, :]), flat(buf[:, 2 * i:2 * i + 2, :]), 0.5,
                                                 flat(hH[:, 2 * i:2 * i + 2, :]).bitcast(F32), ALU.mult,
                                                 ALU.subtract).then_inc(m_lo, 1)
                ada_work(l, n)

            def ada_work(l, n):
                if n in ADA_STEPS:
                    a = ADA_STEPS.index(n)
                    if a < ADA_NEXT:
                        ada_step(l, a)
                    else:
                        with dve.If(l < LAYERS - 1):
                            ada_step(l, a)
                for at, q in ADA_REDUCE_AT.items():
                    if at + 1 == n and ADA_PARTS[q] < 2:
                        with dve.If(l < LAYERS - 1):
                            ada_end(ADA_PARTS[q], l * 6 + 3 + q, vec_all[:, LAYERS - 1, :])
                    elif at + 1 == n:
                        ada_end(ADA_PARTS[q], l * 6 + 3 + q, vec)
                        if q == 2:
                            dve.wait_ge(mi_read, l * 6 + 3 + q)
                            link(dve.scalar_tensor_tensor(gs[:, 1, :], mod[:, 4 * DT:5 * DT], 1.0, vec[:, V_N2:V_N2 + DT],
                                                          ALU.add, ALU.mult))

            def up_step(l, n, r=0):
                i, b = divmod(n - UP, 2)
                u = PB_UP + n - UP
                pb, dst = PB[u % 2], (ca, cb)[b]
                tap = lambda k, t: vec[:, bass.ds(V_FW + k * 2 * FT + b * FT + 2 * i + t + 4 * r, 1)]
                if b == 1:
                    dve.wait_ge(th_ready, l * (FT // 2) + i + 1 + 2 * r)
                    link(dve.scalar_tensor_tensor(flat(gy[:, :, :]), flat(th[:, :, :]), 1.0, flat(ca[:, :, :]), ALU.add, ALU.mult))
                dve.wait_ge(tap_ready, l * 22 + n - UP + 1 + 4 * r)
                for k in (1, 0):
                    lag = FTAPS - 1 - k
                    for t in range(2):
                        ins = dve.scalar_tensor_tensor(dst[:, t, lag:], pb[:, t * T:(t + 1) * T - lag], tap(k, t), dst[:, t, lag:],
                                                       ALU.mult, ALU.add)
                        if (k, t) != (0, 1):
                            link(ins, behind=1)
                ins.then_inc(pb_read[u % 2], 1)
                dve.wait_ge(pb_read[u % 2], FREE + l * (PB_USES // 2) + u // 2 + 1 + 2 * r)
                if b == 1:
                    dve.scalar_tensor_tensor(flat(gy[:, :, :]), flat(gy[:, :, :]), 0.5, flat(cb[:, :, :]), ALU.mult,
                                             ALU.mult).then_inc(gy_ready, 1)
                low(l, n + 2, r)
                if b == 1:
                    dve.wait_ge(g_hi, l * (FT // 2) + i + 1 + 2 * r)
                    dve.tensor_tensor(flat(gL[:, bass.ds(2 * i + 4 * r, 2), :]), flat(gy[:, :, :]),
                                      flat(gH[:, bass.ds(2 * i + 4 * r, 2), :]).bitcast(F32), ALU.subtract).then_inc(g_lo, 1)

            def flush_vectors(l):
                link(dve.tensor_copy(vec[:, :], vec_all[:, l, :]))
                dve.tensor_scalar_mul(vec[:, V_CW:V_CW + ROWS_B], vec[:, V_CW:V_CW + ROWS_B], 0.5)
                dve.tensor_scalar_mul(half_b[:, :], vec[:, V_LNB:V_LNB + CT], 0.5)
                dve.tensor_scalar(sub_g[:, :], vec[:, V_SUB:V_SUB + 1], vec[:, V_LAM + 1:V_LAM + 2], None, ALU.mult)
                dve.tensor_copy(lam_now[:, :], lamb[:, 1, bass.ds(l, 1)])
                dve.wait_ge(mi_read, l * 6 + 2)
                link(dve.scalar_tensor_tensor(gs[:, 0, :], mod[:, DT:2 * DT], 1.0, vec[:, V_N1:V_N1 + DT], ALU.add, ALU.mult))

            dve.wait_ge(s_table, 1)
            low(0, 0)
            ada_end(1, 2, vec_all[:, 0, :])
            before_loop = chain.n
            chain.n = 0
            with dve.Fori(0, LAYERS) as l:
                chain.base = l * V_LINKS + before_loop
                flush_vectors(l)
                norm(l, 0)
                low(l, 1)
                for n in range(WO):
                    mixer_step(l, n)
                for n in range(WO, UP):
                    low(l, n + 2)
                    u = PB_WO + n - WO
                    dve.wait_ge(pb_full, l * PB_USES + u + 1)
                    for t in range(2):
                        k = 2 * (n - WO) + t
                        ins = dve.scalar_tensor_tensor(xT[:, k, :], PB[u % 2][:, t * T:(t + 1) * T],
                                                       mod[:, 2 * DT + k:2 * DT + k + 1], xT[:, k, :], ALU.mult, ALU.add)
                    ins.then_inc(pb_read[u % 2], 1)
                    ada_work(l, n)
                norm(l, 1)
                dve.wait_ge(mi_full, 2 + l * 6 + ADA_LOOP // ADA_PART)
                dve.memset(acc[:, :], 0.0).then_inc(acc_clear, 1)
                ahead = chain.n
                chain.n = 0
                with dve.Fori(0, UP_LOOPS) as r:
                    chain.base = l * V_LINKS + before_loop + ahead + r * V_LINKS_UP
                    for j in range(4):
                        up_step(l, UP + j, r)
                        if j == 2:
                            ada_step(l, ADA_LOOP, r)
                assert chain.n == V_LINKS_UP, chain.n
                chain.n = ahead + UP_LOOPS * V_LINKS_UP
                chain.base = l * V_LINKS + before_loop
                for n in range(UP + 4 * UP_LOOPS, DOWN):
                    up_step(l, n)
                    ada_work(l, n)
                for n in range(DOWN, CHUNKS):
                    if n + 2 < CHUNKS:
                        low(l, n + 2)
                    ada_work(l, n)
                with dve.If(l < LAYERS - 1):
                    low(l + 1, 0)
                dve.wait_ge(mi_read, l * 6 + 6)
                for k in range(DT):
                    if k == DT - 2:
                        dve.wait_ge(down_used, RAW + (l + 1) * (FT // 2))
                    elif k % 2 == 0:
                        dve.wait_ge(down_done, l * 3 + k // 2 + 1)
                    dve.scalar_tensor_tensor(xT[:, k, :], DN[k // 2][:, (k % 2) * T:(k % 2 + 1) * T],
                                             mod[:, 5 * DT + k:5 * DT + k + 1], xT[:, k, :], ALU.mult,
                                             ALU.add).then_inc(x_ready, 1)
                ada_work(l, CHUNKS)
                assert chain.n == V_LINKS, chain.n

            chain.base, chain.n = LAYERS * V_LINKS + before_loop, 0
            dve.wait_ge(st_read, FREE + LAYERS * len(ST_USES) + 1)
            link(dve.reciprocal(rdev[:, 0:T], rdev[:, 0:T]))
            for k in range(DT):
                dve.scalar_tensor_tensor(buf[:, k, :], xT[:, k, :], fin_g[:, k:k + 1], rdev[:, 0:T], ALU.mult,
                                         ALU.mult).then_inc(fin_y, 1)
            for a in range(2):
                dve.wait_ge(out_turned, 2 * a + 1)
                dve.tensor_copy(flat(xn[:, 4 * a:4 * a + 2, :]), OUT[a][0][:, :]).then_inc(out_ready[a], 1)

        @block.tensor
        def _(pe):
            def after(s, count):
                pe.wait_ge(s, count)

            after(s_cst, 16)
            after(s_cvec, 32)
            pe.transpose(MI[:, 0:2 * DT], rows[0:2 * DT, 8, :], ident[0:2 * DT, 0:2 * DT]).then_inc(s_vtr, 1)
            after(s_x, 16)
            x_rows = xn[:, :, :].rearrange("p (a k) t -> p a (k t)", a=2)
            for b in range(4):
                for k in (2 * b, 2 * b + 1):
                    for a in range(2):
                        ins = pe.transpose(DN[b][:, (k % 2) * T + a * P:(k % 2) * T + (a + 1) * P],
                                           x_rows[:, a, k * P:(k + 1) * P], ident)
                ins.then_inc(s_xtr, 1)
            after(s_vec, 16 * VEC_LOADS)
            for l in range(LAYERS):
                for q, count in enumerate((ROWS_A, ROWS_B, 4 * FT, 2 * FT)):
                    ins = pe.transpose(PB[l][:, q * P:q * P + count], rows[0:count, 4 * l + q, :], ident[0:count, 0:count])
                ins.then_inc(s_vtr, 1)
            after(s_ones, 1)
            after(s_vt, 1)

            def reduce_ada(acc=acc):
                for m in range(DT):
                    ins = pe.matmul(MI[:, m:m + 1], acc[:, m * P:(m + 1) * P], ones[:, 0:1], start=True, stop=True)
                ins.then_inc(mi_full, 1)

            def norm_sum(l, which):
                after(st_read, FREE + l * len(ST_USES) + ST_USES.index(("N1", "N2")[which]))
                for k in range(DT):
                    after(sq_ready, l * 2 * DT + which * DT + k + 1)
                    ins = pe.matmul(ST[:, 0:T], ones[:, :], buf[:, k, :], start=(k == 0), stop=(k == DT - 1))
                ins.then_inc(st_full, 1)

            for part in range(2):
                if part == 1:
                    norm_sum(0, 0)
                after(ada_used, ADA_PART * (part + 1))
                if part:
                    after(mi_read, part)
                reduce_ada((acc, acc_pre)[part])
            after(s_const, 1)

            def split_ready(l, n, r=0):
                after(w_lo[n % RAW], l * (CHUNKS // RAW) + n // RAW + 1 + r)
                after(w_lo_pool[n % RAW], l * (CHUNKS // RAW) + n // RAW + 1 + r)
                return wH[n % RAW], wL[n % RAW]

            def pb_free(l, u, r=0):
                after(pb_read[u % 2], FREE + l * (PB_USES // 2) + u // 2 + 2 * r)
                return PB[u % 2]

            def free(l, s, uses, use):
                after(s, FREE + l * len(uses) + uses.index(use))

            def blocks(out, wh, wl, at, m, kt, xh, xl, first=True, last=True, ready=None):
                for k in range(kt):
                    if ready is not None:
                        after(*ready(k))
                    a, b = at(wh, k), at(wl, k)
                    pe.matmul(out, a, xh(k), start=first and k == 0, stop=False, skip_group_check=True)
                    pe.matmul(out, a, xl(k), start=False, stop=False, skip_group_check=True)
                    ins = pe.matmul(out, b, xh(k), start=False, stop=last and k == kt - 1, skip_group_check=True)
                return ins

            def cols(width, c0, m):
                return lambda w, k: w[:, k * width + c0:k * width + c0 + m]

            def pair(pb, wh, wl, width, c0, kt, xh, xl, ready=None):
                for t in range(2):
                    ins = blocks(pb[:, t * T:(t + 1) * T], wh, wl, cols(width, c0 + t * P, P), P, kt, xh, xl,
                                 ready=ready if t == 0 else None)
                return ins

            hh, hl = (lambda k: hH[:, k, :]), (lambda k: hL[:, k, :])

            def statistic(l, use):
                if use == "LAT":
                    for u in range(3):
                        after(pb_read[u % 2], FREE + l * (PB_USES // 2) + u // 2 + 1)
                    sums = [(latq[:, 0:QT, :], QT, 0), (latq[:, QT:QT + KVT, :], KVT, T)]
                elif use in ("SUB0", "SUB1"):
                    i = int(use[3])
                    after(ob_read, FREE + l * len(OB_USES) + OB_USES.index(("PD1", "PD3")[i]) + 1)
                    sums = None
                elif use == "LNS":
                    after(conv_done, l + 1)
                    sums = [(cv[:, :, :], CT, 0)]
                else:
                    after(cen_sq, l + 1)
                    sums = [(latq[:, 0:CT, :], CT, 0)]
                free(l, st_read, ST_USES, use)
                if sums is None:
                    pe.matmul(ST[:, :], ones[:, :], oBq[:, 2 * i:2 * i + 2, :].rearrange("p k t -> p (k t)"), start=True,
                              stop=True).then_inc(st_full, 1)
                    return
                for src, kt, at in sums:
                    for k in range(kt):
                        ins = pe.matmul(ST[:, at:at + T], ones[:, :], src[:, k, :], start=(k == 0), stop=(k == kt - 1))
                ins.then_inc(st_full, 1)

            def h_part(l, which):
                return lambda k: (h_lo, l * 2 * DT + which * DT + k + 1)

            def attention(l, n):
                if n in VALUES_AT:
                    use = VALUES_AT[n]
                    before = "T" + use[1:]
                    after(tr_read, FREE + l * len(TR_USES) + TR_USES.index(before) + 1)
                    free(l, ob_read, OB_USES, use)
                    if use[1] == "D":
                        i, h = divmod(int(use[2]), 2)
                        v = [vD[i][:, t, h * P:(h + 1) * P] for t in range(2)]
                    else:
                        v = [vM[int(use[2]) % 2][:, t, :] for t in range(2)]
                    pe.matmul(OB[:, 0:T], v[0], PT[:, 0:T], start=True, stop=False, skip_group_check=True)
                    pe.matmul(OB[:, P:T], v[1], PT[:, T:T + P], start=False, stop=True,
                              skip_group_check=True).then_inc(ob_full, 1)
                if n in TRANSPOSE_AT:
                    use = TRANSPOSE_AT[n]
                    m = 1 if use[1] == "M" and use[3] == "B" else 0
                    after(w_ready, l * len(SC_USES) + SC_USES.index(use[1:3]) + 1)
                    free(l, tr_read, TR_USES, use)
                    for b in range(3):
                        ins = pe.transpose(TR[:, b * P:(b + 1) * P], W[:, m, b * P:(b + 1) * P], ident)
                    ins.then_inc(tr_full, 1)
                for use in ROTATE_AT.get(n, ()):
                    free(l, tr_read, TR_USES, use)
                    if use == "Rkr":
                        after(pb_read[1], FREE + l * (PB_USES // 2) + 2)
                        ins = pe.matmul(TR[0:96, 0:T], cst[0:96, C_RM:C_RM + 96], krope[0:96, :], start=True, stop=True)
                    elif use[1] == "M":
                        u = PB_MLA + 5 * int(use[2])
                        after(pb_read[u % 2], FREE + l * (PB_USES // 2) + u // 2 + 1)
                        ins = pe.matmul(TR[0:96, :], cst[0:96, C_RM:C_RM + 96],
                                        qraw[0:96, :, :].rearrange("p k t -> p (k t)"), start=True, stop=True)
                    else:
                        u = PB_DIFF + 4 * int(use[2]) + (use[1] == "k")
                        after(pb_read[u % 2], FREE + l * (PB_USES // 2) + u // 2 + 1)
                        src = (qraw, kraw)[use[1] == "k"]
                        ins = pe.matmul(TR[:, :], cst[:, C_RD:C_RD + P], src[:, :, :].rearrange("p k t -> p (k t)"),
                                        start=True, stop=True)
                    ins.then_inc(tr_full, 1)
                if n in SCORES_AT:
                    use = SCORES_AT[n]
                    h = int(use[1])
                    after(roped, l * 8 + (2 * (h // 2 + 1) if use[0] == "D" else 4 + h + 1))
                    if use[0] == "M":
                        u = PB_MLA + 5 * h + 2
                        after(pb_read[u % 2], FREE + l * (PB_USES // 2) + u // 2 + 1)
                    free(l, e_ready, SC_USES, use)
                    for m in range(2):
                        if use[0] == "D":
                            q, k = (s[m * HD:(m + 1) * HD, h % 2, :] for s in (qD, kD))
                        else:
                            q, k = (s[0:96, m, :] for s in (qM, kM))
                        pe.matmul(SC[m][:, 0:384], identb[:, :], maskb[:, :], start=True, stop=False, skip_group_check=True)
                        pe.matmul(SC[m][:, 0:128], q[:, 0:P], k[:, 0:P], start=False, stop=False, skip_group_check=True)
                        ins = pe.matmul(SC[m][:, 128:384], q[:, P:T], k[:, :], start=False, stop=True, skip_group_check=True)
                    ins.then_inc(sc_full, 1)

            def reduce_ada_at(l, n):
                q = ADA_REDUCE_AT.get(n)
                if q is None:
                    return

                def go():
                    after(ada_used, ADA_FIRST + l * ADA_CHUNKS + ADA_PART * (q + 1))
                    after(mi_read, l * 6 + 2 + q)
                    reduce_ada()

                if ADA_PARTS[q] < 2:
                    with pe.If(l < LAYERS - 1):
                        go()
                else:
                    go()

            def chunk(l, n, r=0):
                wh, wl = split_ready(l, n, r)
                if n < LAT + 3:
                    pb = pb_free(l, n)
                    if n < 2:
                        ins = pair(pb, wh, wl, 256, 0, DT, hh, hl, ready=h_part(l, 0) if n == 0 else None)
                        ins.then_inc(pb_full, 1)
                    else:
                        blocks(pb[:, 0:T], wh, wl, cols(P + ROPE, 0, P), P, DT, hh, hl).then_inc(pb_full, 1)
                        pb = pb_free(l, 3)
                        blocks(pb[0:96, 0:T], wh, wl, cols(P + ROPE, P - NOPE, 96), 96, DT, hh, hl).then_inc(pb_full, 1)
                elif n < MLA:
                    i, what = divmod(n - DIFF, 5)
                    if what == 2:
                        free(l, ob_read, OB_USES, f"V{i}")
                        for t in range(2):
                            o = OB[:, t * 256:(t + 1) * 256]
                            for k in range(DT):
                                xh, xl = (x_[:, k, t * P:(t + 1) * P] for x_ in (hH, hL))
                                a, b = (w[:, k * 256:(k + 1) * 256] for w in (wh, wl))
                                pe.matmul(o, xh, a, start=(k == 0), stop=False)
                                pe.matmul(o, xl, a, start=False, stop=False)
                                ins = pe.matmul(o, xh, b, start=False, stop=(k == DT - 1))
                        ins.then_inc(ob_full, 1)
                    else:
                        u = PB_DIFF + 4 * i + (what if what < 2 else what - 1)
                        pair(pb_free(l, u), wh, wl, 256, 0, DT, hh, hl).then_inc(pb_full, 1)
                elif n < OUTS:
                    p, what = divmod(n - MLA, 5)
                    u = PB_MLA + 5 * p + what
                    lh, ll = (lambda k: latH[:, k, :]), (lambda k: latL[:, k, :])
                    if what == 0:
                        after(lat_lo, l + 1)
                        pb = pb_free(l, u)
                        for j in range(2):
                            ins = blocks(pb[0:96, j * T:(j + 1) * T], wh, wl, cols(192, 96 * j, 96), 96, QT, lh, ll)
                        ins.then_inc(pb_full, 1)
                    elif what == 2:
                        lh, ll = (lambda k: latH[:, QT + k, :]), (lambda k: latL[:, QT + k, :])
                        pair(pb_free(l, u), wh, wl, 256, 0, KVT, lh, ll).then_inc(pb_full, 1)
                        free(l, ob_read, OB_USES, f"VM{p}")
                        for t in range(2):
                            o = OB[:, t * P:(t + 1) * P].rearrange("p (h d) -> p h d", h=2)
                            for k in range(KVT):
                                xh, xl = (x_[:, QT + k, t * P:(t + 1) * P] for x_ in (latH, latL))
                                a, b = (w[:, k * 256:(k + 1) * 256].rearrange("p (h d) -> p h d", h=2)[:, :, NOPE:]
                                        for w in (wh, wl))
                                pe.matmul(o, xh, a, start=(k == 0), stop=False)
                                pe.matmul(o, xl, a, start=False, stop=False)
                                ins = pe.matmul(o, xh, b, start=False, stop=(k == KVT - 1))
                        ins.then_inc(ob_full, 1)
                    else:
                        pair(pb_free(l, u), wh, wl, 256, 0, DT, hh, hl).then_inc(pb_full, 1)
                elif n < WO:
                    b, half = divmod(n - OUTS, 2)
                    if b == 0:
                        after(sub_lo, 2 * l + 2)
                    elif b == 1:
                        after(ln_lo, l + 1)
                    else:
                        after(ob_read, FREE + (l + 1) * len(OB_USES))
                    oh, ol = ((oBH, oBL), (uH, uL), (oAH, oAL))[b]
                    for v in range(2):
                        u = PB_OUTS + 2 * (n - OUTS) + v
                        pair(pb_free(l, u), wh, wl, 512, 256 * v, 4, (lambda k: oh[:, k, :]),
                             (lambda k: ol[:, k, :])).then_inc(pb_full, 1)
                elif n < UP:
                    pair(pb_free(l, PB_WO + n - WO), wh, wl, 256, 0, DT, hh, hl,
                         ready=(lambda k: (m_lo, l * 4 + k // 2 + 1)) if n == WO else None).then_inc(pb_full, 1)
                elif n < DOWN:
                    pair(pb_free(l, PB_UP + n - UP, r), wh, wl, 256, 0, DT, hh, hl,
                         ready=h_part(l, 1) if n == UP else None).then_inc(pb_full, 1)
                else:
                    i = n - DOWN
                    after(g_lo, l * (FT // 2) + i + 1)
                    for k in range(DT):
                        ins = blocks(DN[k // 2][:, (k % 2) * T:(k % 2 + 1) * T], wh, wl, cols(1024, k * P, P), P, 2,
                                     lambda j: gH[:, 2 * i + j, :], lambda j: gL[:, 2 * i + j, :],
                                     first=(i == 0 and k % 2 == 0), last=(n == CHUNKS - 1))
                        if n == CHUNKS - 1 and k in (1, 3, 5):
                            ins.then_inc(down_done, 1)
                    ins.then_inc(down_used, 1)

            with pe.Fori(0, LAYERS) as l:
                for n in range(UP):
                    chunk(l, n)
                    attention(l, n)
                    if n in STATS_AT:
                        statistic(l, STATS_AT[n])
                    reduce_ada_at(l, n)
                    if n == UP - 1:
                        norm_sum(l, 1)
                with pe.Fori(0, UP_LOOPS) as r:
                    for j in range(4):
                        chunk(l, UP + j, r)
                for n in range(UP + 4 * UP_LOOPS, CHUNKS):
                    chunk(l, n)
                    reduce_ada_at(l, n)
                norm_sum(l + 1, 0)

            for a in range(2):
                for b in range(2):
                    after(fin_y, 4 * b + 4)
                    for k in range(4):
                        ins = pe.transpose(OUT[a][b][:, k * P:(k + 1) * P], buf[:, 4 * b + k, a * P:(a + 1) * P], ident)
                    ins.then_inc(out_turned, 1)


_INS = ["x", "c", "positions", "ada_w", "ada_b", "norm1_g", "w_in", "q_norm_g", "w_uq", "kv_norm_g", "w_ukv", "w_out_mla",
        "diff_lambda", "diff_subln_g", "w_out_diff", "conv_dw_w", "conv_dw_b", "conv_ln_g", "conv_ln_b", "w_out_conv",
        "w_o", "norm2_g", "w_up", "ffn_conv_w", "ffn_conv_b", "w_down", "final_g"]


def kernel(**inputs):
    import concourse.bacc as bacc
    from concourse.bass_utils import run_bass_kernel_spmd

    nc = bacc.Bacc("TRN2", target_bir_lowering=False, num_devices=1)
    arrays, args = {}, []
    for name in _INS + ["consts"]:
        a = constants() if name == "consts" else np.ascontiguousarray(inputs[name])
        arrays[f"in_{name}"] = a
        args.append(nc.dram_tensor(f"in_{name}", a.shape, mybir.dt.from_np(a.dtype), kind="ExternalInput").ap())
    out = nc.dram_tensor("out_0", (1, T, D), F32, kind="ExternalOutput").ap()
    trunk_kernel(nc, *args, out)
    r = run_bass_kernel_spmd(nc, [arrays], core_ids=[0])
    return r.results[0]["out_0"]
```
